# Optimizing a Trainium2 kernel written in Bass

```python
import math
import jax
import jax.numpy as jnp
from jax import lax
import numpy as np

D_MODEL = 1024
BATCH = 1
SEQ = 512
DEPTH = 2

GRID_W = 64
CTX_LEN = 256
HEAD_DIM = 64
A_HEADS = 4
A_VDIM = 2 * HEAD_DIM
B_HEADS = 8
B_KV_HEADS = 2
C_HEADS = D_MODEL // HEAD_DIM
NA_WIN_H = 8
NA_WIN_W = 16
RPB_H = 2 * NA_WIN_H - 1
RPB_W = 2 * NA_WIN_W - 1
N_GROUPS = 4
EXPERTS_PER_GROUP = 8
N_EXPERTS = N_GROUPS * EXPERTS_PER_GROUP
TOP_K_INNER = 2
D_EXPERT = 512
MOE_BLOCK = 128
Q_BLOCK = 128
ROPE_THETA = 10000.0
N_EVEN = (DEPTH + 1) // 2
N_ODD = DEPTH // 2
DN_ALPHA = (2.0 * DEPTH) ** 0.25
DN_BETA = (8.0 * DEPTH) ** -0.25
A_QK = A_HEADS * 2 * HEAD_DIM
A_V = A_HEADS * A_VDIM
B_Q = B_HEADS * HEAD_DIM
B_KV = B_KV_HEADS * HEAD_DIM
EVEN_IN = 2 * A_QK + A_V + B_Q + 2 * B_KV
EVEN_OUT = A_V + B_Q
C_WIDTH = C_HEADS * HEAD_DIM
ODD_IN = 3 * C_WIDTH

kernel_name = "hybrid_diffattn_gqa_natten_hmoe_deepnorm"

def layer_norm(x, g, b, eps=1e-6):
    xf = x.astype(jnp.float32)
    mu = jnp.mean(xf, axis=-1, keepdims=True)
    var = jnp.mean(jnp.square(xf - mu), axis=-1, keepdims=True)
    return ((xf - mu) * lax.rsqrt(var + eps) * g.astype(jnp.float32) + b.astype(jnp.float32)).astype(x.dtype)

def rms_norm(x, g, eps=1e-6):
    xf = x.astype(jnp.float32)
    ms = jnp.mean(jnp.square(xf), axis=-1, keepdims=True)
    return (xf * lax.rsqrt(ms + eps) * g.astype(jnp.float32)).astype(x.dtype)

def softmax_f32(s):
    return jax.nn.softmax(s.astype(jnp.float32), axis=-1)

def axial_rope_tables(n_tokens):
    t = jnp.arange(n_tokens, dtype=jnp.int32)
    row = (t // GRID_W).astype(jnp.float32)
    col = (t % GRID_W).astype(jnp.float32)
    half = HEAD_DIM // 2
    inv = ROPE_THETA ** (-jnp.arange(0, half, 2, dtype=jnp.float32) / half)
    ang_r = row[:, None] * inv[None, :]
    ang_c = col[:, None] * inv[None, :]
    ang = jnp.concatenate([ang_r, ang_r, ang_c, ang_c], axis=-1)
    return jnp.cos(ang), jnp.sin(ang)

def rotate_axial(x):
    q = HEAD_DIM // 4
    x1, x2, x3, x4 = x[..., :q], x[..., q:2 * q], x[..., 2 * q:3 * q], x[..., 3 * q:]
    return jnp.concatenate([-x2, x1, -x4, x3], axis=-1)

def apply_rope(x, cos, sin):
    shape = (1, x.shape[1]) + (1,) * (x.ndim - 3) + (HEAD_DIM,)
    xf = x.astype(jnp.float32)
    return (xf * cos.reshape(shape) + rotate_axial(xf) * sin.reshape(shape)).astype(x.dtype)

def neighbourhood_tables(n_tokens):
    rows = n_tokens // GRID_W
    kh = min(NA_WIN_H, rows)
    kw = NA_WIN_W
    t = jnp.arange(n_tokens, dtype=jnp.int32)
    r = t // GRID_W
    c = t % GRID_W
    rs = jnp.clip(r - kh // 2, 0, rows - kh)
    cs = jnp.clip(c - kw // 2, 0, GRID_W - kw)
    kr = rs[:, None, None] + jnp.arange(kh, dtype=jnp.int32)[None, :, None]
    kc = cs[:, None, None] + jnp.arange(kw, dtype=jnp.int32)[None, None, :]
    idx = (kr * GRID_W + kc).reshape(n_tokens, kh * kw)
    bidx = ((kr - r[:, None, None] + (NA_WIN_H - 1)) * RPB_W
            + (kc - c[:, None, None] + (NA_WIN_W - 1))).reshape(n_tokens, kh * kw)
    return idx, bidx

def to_blocks(a):
    b, n = a.shape[:2]
    return jnp.swapaxes(a.reshape((b, n // Q_BLOCK, Q_BLOCK) + a.shape[2:]), 0, 1)

def from_blocks(o):
    nb, b, q = o.shape[:3]
    return jnp.swapaxes(o, 0, 1).reshape((b, nb * q) + o.shape[3:])

def diff_attn_core(q, k, v, lam, lam_init, sub_g):
    b, nq = q.shape[:2]
    s = jnp.einsum('bqhmd,bkhmd->bhmqk', q, k) * (HEAD_DIM ** -0.5)
    p = softmax_f32(s)
    a = (p[:, :, 0] - lam * p[:, :, 1]).astype(v.dtype)
    o = jnp.einsum('bhqk,bkhe->bqhe', a, v)
    o = rms_norm(o, sub_g) * (1.0 - lam_init)
    return o.reshape(b, nq, A_V)

def gqa_core(q, k, v):
    b, nq = q.shape[:2]
    q = q.reshape(b, nq, B_KV_HEADS, B_HEADS // B_KV_HEADS, HEAD_DIM)
    s = jnp.einsum('bqgrd,bkgd->bgrqk', q, k) * (HEAD_DIM ** -0.5)
    p = softmax_f32(s).astype(v.dtype)
    o = jnp.einsum('bgrqk,bkgd->bqgrd', p, v)
    return o.reshape(b, nq, B_Q)

def even_mixer(h_lat, h_ctx, w_in, w_out, lam_vec, sub_g, qk_g, lam_init, cos, sin, with_ctx):
    b = h_lat.shape[0]
    splits = [A_QK, 2 * A_QK, 2 * A_QK + A_V, 2 * A_QK + A_V + B_Q, 2 * A_QK + A_V + B_Q + B_KV]

    def project(h):
        s = h.shape[1]
        aq, ak, av, bq, bk, bv = jnp.split(h @ w_in, splits, axis=-1)
        aq = aq.reshape(b, s, A_HEADS, 2, HEAD_DIM)
        ak = ak.reshape(b, s, A_HEADS, 2, HEAD_DIM)
        av = av.reshape(b, s, A_HEADS, A_VDIM)
        bq = rms_norm(bq.reshape(b, s, B_HEADS, HEAD_DIM), qk_g[0])
        bk = rms_norm(bk.reshape(b, s, B_KV_HEADS, HEAD_DIM), qk_g[1])
        bv = bv.reshape(b, s, B_KV_HEADS, HEAD_DIM)
        return aq, ak, av, bq, bk, bv

    aq_l, ak_l, av_l, bq_l, bk_l, bv_l = project(h_lat)
    aq_l = apply_rope(aq_l, cos, sin)
    ak_l = apply_rope(ak_l, cos, sin)
    bq_l = apply_rope(bq_l, cos, sin)
    bk_l = apply_rope(bk_l, cos, sin)
    aq_c, ak_c, av_c, bq_c, bk_c, bv_c = project(h_ctx)
    lamf = lam_vec.astype(jnp.float32)
    lam = jnp.exp(jnp.sum(lamf[0] * lamf[1])) - jnp.exp(jnp.sum(lamf[2] * lamf[3])) + lam_init
    ak_all = jnp.concatenate([ak_c, ak_l], axis=1)
    av_all = jnp.concatenate([av_c, av_l], axis=1)
    bk_all = jnp.concatenate([bk_c, bk_l], axis=1)
    bv_all = jnp.concatenate([bv_c, bv_l], axis=1)

    def block(args):
        aq_b, bq_b = args
        return jnp.concatenate([diff_attn_core(aq_b, ak_all, av_all, lam, lam_init, sub_g),
                                gqa_core(bq_b, bk_all, bv_all)], axis=-1)

    out_l = from_blocks(lax.map(block, (to_blocks(aq_l), to_blocks(bq_l)))) @ w_out
    if not with_ctx:
        return out_l, None
    out_c = jnp.concatenate([diff_attn_core(aq_c, ak_c, av_c, lam, lam_init, sub_g),
                             gqa_core(bq_c, bk_c, bv_c)], axis=-1) @ w_out
    return out_l, out_c

def odd_mixer(h_lat, h_ctx, w_in, w_out, rpb, nbr_idx, bias_idx, with_ctx):
    b = h_lat.shape[0]

    def project(h):
        s = h.shape[1]
        q, k, v = jnp.split(h @ w_in, 3, axis=-1)
        return (q.reshape(b, s, C_HEADS, HEAD_DIM), k.reshape(b, s, C_HEADS, HEAD_DIM),
                v.reshape(b, s, C_HEADS, HEAD_DIM))

    q_l, k_l, v_l = project(h_lat)
    q_c, k_c, v_c = project(h_ctx)
    rpb_flat = rpb.reshape(C_HEADS, RPB_H * RPB_W)
    scale = HEAD_DIM ** -0.5
    n_nbr = nbr_idx.shape[1]

    def block(args):
        q_b, idx_b, bidx_b = args
        k_nb = k_l[:, idx_b]
        v_nb = v_l[:, idx_b]
        s_nb = jnp.einsum('bqhd,bqnhd->bhqn', q_b, k_nb) * scale + rpb_flat[:, bidx_b][None]
        s_cx = jnp.einsum('bqhd,bkhd->bhqk', q_b, k_c) * scale
        p = softmax_f32(jnp.concatenate([s_nb, s_cx], axis=-1)).astype(v_l.dtype)
        o = (jnp.einsum('bhqn,bqnhd->bqhd', p[..., :n_nbr], v_nb)
             + jnp.einsum('bhqk,bkhd->bqhd', p[..., n_nbr:], v_c))
        return o.reshape(b, q_b.shape[1], C_WIDTH)

    nb = nbr_idx.shape[0] // Q_BLOCK
    out_l = from_blocks(lax.map(block, (to_blocks(q_l),
                                        nbr_idx.reshape(nb, Q_BLOCK, n_nbr),
                                        bias_idx.reshape(nb, Q_BLOCK, n_nbr)))) @ w_out
    if not with_ctx:
        return out_l, None
    s = jnp.einsum('bqhd,bkhd->bhqk', q_c, k_c) * scale
    p = softmax_f32(s).astype(v_c.dtype)
    out_c = jnp.einsum('bhqk,bkhd->bqhd', p, v_c).reshape(b, q_c.shape[1], C_WIDTH) @ w_out
    return out_l, out_c

def hier_moe(h, router_g, router_e, w1, w3, w2):
    n_tok = h.shape[0]
    lg = (h @ router_g).astype(jnp.float32)
    pg = jax.nn.softmax(lg, axis=-1)
    g_star = jnp.argmax(lg, axis=-1).astype(jnp.int32)
    p_top = jnp.take_along_axis(pg, g_star[:, None], axis=1)
    le = (h @ router_e).astype(jnp.float32).reshape(n_tok, N_GROUPS, EXPERTS_PER_GROUP)
    le_g = jnp.take_along_axis(le, g_star[:, None, None], axis=1)[:, 0]
    top_v, top_i = lax.top_k(le_g, TOP_K_INNER)
    gate = jax.nn.softmax(top_v, axis=-1) * p_top
    expert = g_star[:, None] * EXPERTS_PER_GROUP + top_i.astype(jnp.int32)
    n_assign = n_tok * TOP_K_INNER
    e_flat = expert.reshape(-1)
    tok_flat = jnp.repeat(jnp.arange(n_tok, dtype=jnp.int32), TOP_K_INNER)
    w_flat = gate.reshape(-1)
    order = jnp.argsort(e_flat)
    e_s, tok_s, w_s = e_flat[order], tok_flat[order], w_flat[order]
    counts = jnp.zeros((N_EXPERTS,), jnp.int32).at[e_flat].add(1)
    starts = jnp.cumsum(counts) - counts
    padded = (counts + MOE_BLOCK - 1) // MOE_BLOCK * MOE_BLOCK
    pad_ends = jnp.cumsum(padded)
    pad_starts = pad_ends - padded
    dest = pad_starts[e_s] + jnp.arange(n_assign, dtype=jnp.int32) - starts[e_s]
    n_blocks = (n_assign + MOE_BLOCK - 1) // MOE_BLOCK + N_EXPERTS
    n_rows = n_blocks * MOE_BLOCK
    row_tok = jnp.zeros((n_rows,), jnp.int32).at[dest].set(tok_s)
    row_w = jnp.zeros((n_rows,), jnp.float32).at[dest].set(w_s)
    block_exp = jnp.minimum(jnp.searchsorted(pad_ends, jnp.arange(n_blocks, dtype=jnp.int32) * MOE_BLOCK,
                                             side='right'), N_EXPERTS - 1).astype(jnp.int32)

    def expert_block(args):
        tok_b, e = args
        xb = h[tok_b]
        return (jax.nn.silu(xb @ w1[e]) * (xb @ w3[e])) @ w2[e]

    y = lax.map(expert_block, (row_tok.reshape(n_blocks, MOE_BLOCK), block_exp))
    y = y.reshape(n_rows, h.shape[1]) * row_w[:, None].astype(h.dtype)
    return jnp.zeros_like(h).at[row_tok].add(y)

def setup_inputs(seed: int = 0) -> dict:
    key = jax.random.key(seed)
    ks = jax.random.split(key, 21)
    D = D_MODEL

    def nrm(k, shape, scale):
        return jax.random.normal(k, shape, jnp.float32) * scale

    return {
        "x": nrm(ks[0], (BATCH, SEQ, D), 1.0),
        "c": nrm(ks[1], (BATCH, D), 1.0),
        "ctx": nrm(ks[2], (BATCH, CTX_LEN, D), 1.0),
        "c_ctx": nrm(ks[3], (D,), 1.0),
        "w_mod": nrm(ks[4], (DEPTH, D, 6 * D), 0.5 * D ** -0.5),
        "b_mod": nrm(ks[5], (DEPTH, 6 * D), 0.01),
        "ln_g": 1.0 + nrm(ks[6], (DEPTH, 2, D), 0.02),
        "ln_b": nrm(ks[7], (DEPTH, 2, D), 0.01),
        "w_in_even": nrm(ks[8], (N_EVEN, D, EVEN_IN), D ** -0.5),
        "w_out_even": nrm(ks[9], (N_EVEN, EVEN_OUT, D), DN_BETA * EVEN_OUT ** -0.5),
        "diff_lam": nrm(ks[10], (N_EVEN, 4, HEAD_DIM), 0.1),
        "diff_subln_g": 1.0 + nrm(ks[11], (N_EVEN, A_VDIM), 0.02),
        "gqa_qk_g": 1.0 + nrm(ks[12], (N_EVEN, 2, HEAD_DIM), 0.02),
        "w_in_odd": nrm(ks[13], (N_ODD, D, ODD_IN), D ** -0.5),
        "w_out_odd": nrm(ks[14], (N_ODD, C_WIDTH, D), DN_BETA * C_WIDTH ** -0.5),
        "na_rpb": nrm(ks[15], (N_ODD, C_HEADS, RPB_H, RPB_W), 0.02),
        "router_g": nrm(ks[16], (DEPTH, D, N_GROUPS), D ** -0.5),
        "router_e": nrm(ks[17], (DEPTH, D, N_EXPERTS), D ** -0.5),
        "w1": nrm(ks[18], (DEPTH, N_EXPERTS, D, D_EXPERT), D ** -0.5),
        "w3": nrm(ks[19], (DEPTH, N_EXPERTS, D, D_EXPERT), D ** -0.5),
        "w2": nrm(ks[20], (DEPTH, N_EXPERTS, D_EXPERT, D), DN_BETA * D_EXPERT ** -0.5),
    }

def reference(x, c, ctx, c_ctx, w_mod, b_mod, ln_g, ln_b, w_in_even, w_out_even, diff_lam, diff_subln_g,
              gqa_qk_g, w_in_odd, w_out_odd, na_rpb, router_g, router_e, w1, w3, w2):
    b, n, d = x.shape
    n_ctx = ctx.shape[1]
    cos, sin = axial_rope_tables(n)
    nbr_idx, bias_idx = neighbourhood_tables(n)
    s_c = jax.nn.silu(c)
    s_cc = jax.nn.silu(c_ctx)
    for l in range(DEPTH):
        last = l == DEPTH - 1
        i = l // 2
        mod = (s_c @ w_mod[l] + b_mod[l])[:, None, :]
        mod_c = s_cc @ w_mod[l] + b_mod[l]
        sh1, sc1, g1, sh2, sc2, g2 = jnp.split(mod, 6, axis=-1)
        csh1, csc1, cg1, csh2, csc2, cg2 = jnp.split(mod_c, 6, axis=-1)
        h_l = x * (1.0 + sc1) + sh1
        h_c = ctx * (1.0 + csc1) + csh1
        if l % 2 == 0:
            lam_init = 0.8 - 0.6 * math.exp(-0.3 * l)
            mix_l, mix_c = even_mixer(h_l, h_c, w_in_even[i], w_out_even[i], diff_lam[i], diff_subln_g[i],
                                      gqa_qk_g[i], lam_init, cos, sin, not last)
        else:
            mix_l, mix_c = odd_mixer(h_l, h_c, w_in_odd[i], w_out_odd[i], na_rpb[i], nbr_idx, bias_idx, not last)
        x = layer_norm(DN_ALPHA * x + g1 * mix_l, ln_g[l, 0], ln_b[l, 0])
        if not last:
            ctx = layer_norm(DN_ALPHA * ctx + cg1 * mix_c, ln_g[l, 0], ln_b[l, 0])
        h2_l = (x * (1.0 + sc2) + sh2).reshape(b * n, d)
        if last:
            y_l = hier_moe(h2_l, router_g[l], router_e[l], w1[l], w3[l], w2[l]).reshape(b, n, d)
        else:
            h2_c = (ctx * (1.0 + csc2) + csh2).reshape(b * n_ctx, d)
            y = hier_moe(jnp.concatenate([h2_c, h2_l], axis=0), router_g[l], router_e[l], w1[l], w3[l], w2[l])
            y_l = y[b * n_ctx:].reshape(b, n, d)
            ctx = layer_norm(DN_ALPHA * ctx + cg2 * y[:b * n_ctx].reshape(b, n_ctx, d), ln_g[l, 1], ln_b[l, 1])
        x = layer_norm(DN_ALPHA * x + g2 * y_l, ln_g[l, 1], ln_b[l, 1])
    return x


_drawn_inputs = setup_inputs


def setup_inputs(seed=0):
    import zlib

    import numpy as np

    out = dict(_drawn_inputs(seed))
    spreads = {}
    factors = {'ctx': 3.481,
     'b_mod': 8.0,
     'ln_b': 2.699,
     'diff_lam': 8.0,
     'diff_subln_g': 115.51,
     'gqa_qk_g': 38.775,
     'na_rpb': 200.0}
    for name, (base, spread) in spreads.items():
        noise = np.random.default_rng([zlib.crc32(name.encode()), seed]).standard_normal(out[name].shape)
        drawn = base * np.exp(spread * noise) if base else spread * noise
        out[name] = jnp.asarray(drawn.astype(out[name].dtype))
    for name, factor in factors.items():
        out[name] = (out[name] * factor).astype(out[name].dtype)
    return out
```

```python
import math
from contextlib import ExitStack

import concourse.bass as bass
from concourse import mybir

P = 128
D = 1024
KT = D // P
SEQ, CTX = 512, 256
NTOK = CTX + SEQ
NT = NTOK // P
NCT = CTX // P
DEPTH = 2
MOE_TOK = [NTOK, SEQ]
GRID_W, ROWS_N, WIN_W = 64, SEQ // 64, 16
RPB_H, RPB_W = 15, 31
HD = 64
NE, NG, EPG = 32, 4, 8
DE = 512
EVEN_IN, ODD_IN = 2304, 3072
ALPHA = (2.0 * DEPTH) ** 0.25
LAM_INIT = 0.8 - 0.6 * math.exp(0.0)
EPS = 1e-6
BIG_NEG = -1.0e30
CAP = 96
JMAX = (NTOK - 1) // CAP
NOV = (2 * NTOK - 1) // CAP
NB = NE + NOV
EMPTY = 1 << 20
C_ID, C_TRI, C_ONE, C_IOTA, C_PRIO, C_PRIO4, C_TOK, C_MASK = 0, 128, 256, 384, 416, 448, 452, 458
C_W = 458 + 64
SLOT = 12288
Q0, K0, V0, BK0, BV0, P0, PT0, RS0, RT0, RO0 = 0, 1536, 2304, 3072, 3840, 4608, 7680, 9216, 9728, 10240
WC0 = SLOT
WO0 = SLOT
TA0 = SLOT + 8192
H2T0, TMP0 = TA0, TA0 + 2048


class Steps:

    def __init__(self, eng, sem):
        self.eng, self.sem, self.base, self.n = eng, sem, 0, 0

    def did(self, ins):
        ins.then_inc(self.sem, 1)
        self.n += 1

    def settle(self):
        self.eng.wait_ge(self.sem, self.base + self.n)

    def then(self, ins):
        self.did(ins)
        self.settle()

    def enter(self, i, per):
        self.outer, self.per = self.base + self.n, per
        self.base, self.n = self.outer + i * per, 0

    def leave(self, count):
        assert self.n == self.per, (self.n, self.per)
        self.base, self.n = self.outer + count * self.per, 0


def build(nc, A, out):
    f32, i32 = mybir.dt.float32, mybir.dt.int32
    ALU, ACT, AX = mybir.AluOpType, mybir.ActivationFunctionType, mybir.AxisListType
    ds = bass.ds
    ctx = ExitStack()

    def dram(name, shape, dt=f32):
        return nc.dram_tensor(name, shape, dt).ap()

    mod_d = [dram(f"mod_rows_{l}", [96, P]) for l in range(DEPTH)]
    h2_d = [dram(f"h2_rows_{l}", [MOE_TOK[l], D]) for l in range(DEPTH)]
    tab_d = [dram(f"slot_tokens_{l}", [CAP * NB, 1], i32) for l in range(DEPTH)]
    y_d = [dram(f"expert_rows_{l}", [2 * MOE_TOK[l], D]) for l in range(DEPTH)]
    skew_d = dram("rpb_skewed", [GRID_W * 16 * RPB_H * RPB_W])
    LR = 16 * RPB_H * RPB_W

    with ctx:
        def sb(name, shape, dt=f32):
            return ctx.enter_context(nc.sbuf_tensor(name, shape, dt))

        sems = {}

        def S(name):
            if name not in sems:
                sems[name] = ctx.enter_context(nc.semaphore(name))
            return sems[name]

        X = sb("X", [P, NT, D])
        HT = sb("HT", [P, KT, NTOK])
        OO = sb("OO", [P, NT, D])
        ROWS = sb("ROWS", [P, 8, D])
        BIG = sb("BIG", [P, 2 * SLOT])
        CO = sb("CO", [P, C_W])
        TOKI = sb("TOKI", [P, 2, NT], i32)
        SC = sb("SC", [P, KT, 2])
        MT = sb("MT", [P, DEPTH, 2, 48])
        RW = sb("RW", [P, KT, NG + NE])
        LG = sb("LG", [P, NT, NG + NE])
        SUBG = sb("SUBG", [P, P])
        LAM = sb("LAM", [P, 4])
        NMX = sb("NMX", [P, 4, 4])
        SUM = sb("SUM", [P, 4, 4])
        RCP = sb("RCP", [P, 4, 4])
        MS = sb("MS", [P, 8])
        BN = sb("BN", [P, 2, 6])
        MV = sb("MV", [P, 4])
        MHALF = sb("MHALF", [P, 8])
        GATE = sb("GATE", [P, 2, NT])
        ADI = sb("ADI", [P, 2, NT], i32)
        IX = sb("IX", [P, 2], i32)
        IY = sb("IY", [P, 2], i32)
        OVI = sb("OVI", [1, DEPTH, 20], i32)
        IDX = sb("IDX", [P, NB], i32)
        IDT = sb("IDT", [P, NB], i32)
        PB = ctx.enter_context(nc.psum_tensor("PB", [P, 8, 512], f32))
        PF = PB[:, :, :].rearrange("p b n -> p (b n)")
        HF = HT[:, :, :].rearrange("p k n -> p (k n)")
        OF = OO[:, :, :].rearrange("p k n -> p (k n)")

        ident = CO[:, C_ID:C_ID + P]
        tri = CO[:, C_TRI:C_TRI + P]
        ones = CO[:, C_ONE:C_ONE + P]
        iota = CO[:, C_IOTA:C_IOTA + NE]
        prio = CO[:, C_PRIO:C_PRIO + NE]
        prio4 = CO[:, C_PRIO4:C_PRIO4 + NG]
        colmask = CO[:, C_MASK:C_MASK + GRID_W]

        WM = [BIG[:, 4096 * u:4096 * (u + 1)].rearrange("p (k n) -> p k n", k=KT) for u in range(3)]
        BM = [HF[0:2, :], ROWS[0:2, 0:6, :].rearrange("p a n -> p (a n)")]
        CROW = OF[0:2 * KT, 1056:1184]
        LMV = OF[:, 544:800].rearrange("p (a n) -> p a n", a=4)
        LMT = OF[:, 800:928].rearrange("p (a n) -> p a n", a=2)
        QG = OF[:, 928:1056].rearrange("p (a n) -> p a n", a=2)

        QT = BIG[:, Q0:Q0 + 1536].rearrange("p (s n) -> p s n", s=2)
        KTr, V = BIG[:, K0:K0 + 768], BIG[:, V0:V0 + 768].rearrange("p (t n) -> p t n", t=NT)
        BK, BV = BIG[:, BK0:BK0 + 768], BIG[:, BV0:BV0 + 768].rearrange("p (t n) -> p t n", t=NT)
        PR = BIG[:, P0:P0 + 3072].rearrange("p (u m n) -> p u m n", u=2, m=2)
        PT = BIG[:, PT0:PT0 + 1536].rearrange("p (u j n) -> p u j n", u=2, j=6)
        RS = BIG[:, RS0:RS0 + 512].rearrange("p (u n) -> p u n", u=2)
        RT = BIG[:, RT0:RT0 + 512].rearrange("p (u n) -> p u n", u=2)
        RO = BIG[:, RO0:RO0 + 512].rearrange("p (u n) -> p u n", u=2)
        PR1 = BIG[:, P0:P0 + 1536].rearrange("p (u n) -> p u n", u=2)
        WC = [BIG[:, WC0 + 3072 * u:WC0 + 3072 * (u + 1)].rearrange("p (k n) -> p k n", k=KT) for u in range(2)]
        WO = [BIG[:, WO0 + 4096 * n:WO0 + 4096 * (n + 1)].rearrange("p (k n) -> p k n", k=KT) for n in range(2)]
        TAB = BIG[:, TA0:TA0 + 2304].rearrange("p (a t s n) -> p a t s n", a=3, t=NT, s=2)
        RAW = BIG[:, 9216:9216 + 2 * 480].rearrange("p (s n) -> p s n", s=2)
        GT = BIG[:, 10240:10240 + 2 * 896].rearrange("p (s j n) -> p s j n", s=2, j=14)
        H2T = BIG[:, H2T0:H2T0 + 2048].rearrange("p (u k n) -> p u k n", u=2, k=KT)
        TMP = BIG[:, TMP0:TMP0 + 1024]
        SQ = BIG[:, TMP0 + 1024:TMP0 + 1536]

        W1 = [BIG[:, SLOT * u:SLOT * u + 4096].rearrange("p (k n) -> p k n", k=KT) for u in range(2)]
        W3 = [BIG[:, SLOT * u + 4096:SLOT * u + 8192].rearrange("p (k n) -> p k n", k=KT) for u in range(2)]
        W2 = [BIG[:, SLOT * u + 8192:SLOT * u + 12288].rearrange("p (k n) -> p k n", k=4) for u in range(2)]
        XG = [HF[:, 1024 * u:1024 * (u + 1)] for u in range(2)]
        XT = [HF[:, 2048 + 768 * u:2048 + 768 * (u + 1)].rearrange("p (k n) -> p k n", k=KT) for u in range(2)]
        SG = [HF[:, 3584 + 384 * u:3584 + 384 * (u + 1)].rearrange("p (k n) -> p k n", k=4) for u in range(2)]
        HX = [HF[:, 4352 + 384 * u:4352 + 384 * (u + 1)].rearrange("p (k n) -> p k n", k=4) for u in range(2)]
        YS = [OF[:, 1024 * u:1024 * (u + 1)] for u in range(2)]
        YG = [HF[:, 2048 * u:2048 * (u + 1)].rearrange("p (k n) -> p k n", k=2) for u in range(2)]

        def grid(n, w=NE):
            return OF[:, 2048 + 192 * n:2048 + 192 * n + NT * w].rearrange("p (t e) -> p t e", t=NT)

        ROW_G, ROW_SC, ROW_SH, ROW_LG, ROW_LB = 0, 2, 4, 6, 7

        LAYER0 = dict(cT=12, cTa=12, cTd=12, chosen=1, down_free=NE + 2, down_loaded0=8 * NE, down_loaded1=8 * NE, gexp=1, gmax=1,
                      h2_stored=16 * NT, h2=NT, hTa=NT, hTd=NT, hx=NE, ix=NE, iy=NE, tokens=1, lg_out=NT, lg=NT, mix_used=NT, mix=NT, ranks=1,
                      routed=1, rowsf=64, rows=128, rw_loaded=32, scattered=32 * NT, sg=NE, slots=16, texp=1, top2=1,
                      up1=NE, up_free=NE + 2, up_loaded0=16 * NE, up_loaded1=16 * NE, wo_free=1, wo_loaded=32, xTa=NE, xTd=NE,
                      xT=NT, x_new=NT, xgT=NE, xg0=8 * NE, xg1=8 * NE, y_all=1, y_a=NE, y_d=NE, y_stored0=8 * NE,
                      y_stored1=8 * NE, yg_used=NT, yg0=8 * NT, yg1=8 * NT, ln_ms=NT, ln_root=NT, lnf_ms=NT, lnf_root=NT)

        CREDIT = dict(y_a=1, y_d=1)

        def wait(eng, what, l, n):
            eng.wait_ge(S(what), n + l * LAYER0.get(what, 0) + CREDIT.get(what, 0))

        def lone_wait(eng, sem, n):
            eng.wait_ge(sem, n)
            eng.nop(nofuse=True)

        def overflow(eng, l, body):
            wait(eng, "routed", l, 1)
            n_over = eng.value_load(OVI[0:1, l, 16:17], min_val=0, max_val=NOV)
            prev = eng.value_load(OVI[0:1, 0, 16:17], min_val=0, max_val=NOV) if l else 0
            with eng.Fori(0, NOV) as b:
                with eng.If(b < n_over):
                    body(b, b + prev)

        def m_of(t):
            return 1 if t < NCT else 0

        def mod_row(l, part, m):
            return mod_d[l][48 * m + 8 * part:48 * m + 8 * part + 8, :].rearrange("j n -> (j n)").partition_broadcast(P)

        tiles_of = [list(range(NT)), list(range(NCT, NT))]
        MOE_TILES = tiles_of

        PER_MAP = ("scores", "max", "exp")
        UNIT_STEPS = PER_MAP + ("probs_T", "pt_a", "pt_d", "o", "o_out")

        class Phase:
            def __init__(self, name, iters, units, maps, local):
                self.name, self.iters, self.units, self.maps, self.local = name, iters, units, maps, local
                self.nu = len(units)
                self.before = dict.fromkeys(UNIT_STEPS, 0)

            def s(self, what):
                return S(f"att_{what}" if what in UNIT_STEPS else f"{self.name}_{what}")

            def wait(self, eng, what, n):
                eng.wait_ge(self.s(what), n + (self.before[what] if what in UNIT_STEPS else 0))

            def after(self, other):
                for w in UNIT_STEPS:
                    self.before[w] = other.before[w] + other.iters * other.nu * (other.maps if w in PER_MAP else 1)
                return self

            def nk(self, t):
                return CTX if (t < NCT) else NTOK

            def jt(self, t):
                if self.local:
                    return [2, 3, 4, 5, 0, 1], 4
                return ([0, 1], 1) if t < NCT else ([0, 1, 2, 3, 4, 5], 4)

            def region(self, u, m):
                return 2 * m if self.maps == 2 else 2 * (u % 2)

        PA = Phase("a0", 4, [(t, 0) for t in range(NT)], 2, False)
        PBB = Phase("b0", 4, [(t, s) for s in range(2) for t in range(NT)], 1, False).after(PA)
        PN = Phase("n1", 8, [(t, s) for s in range(2) for t in range(NCT, NT)], 1, True).after(PBB)

        block = ctx.enter_context(nc.Block())

        @block.sync
        def _(sp):
            for l in range(DEPTH):
                wm = A["w_mod"][l].rearrange("(k p) n -> p k n", p=P)
                for i_ in ([None] if l else [0, None]):
                    if i_ == 0:
                        for u in range(3):
                            sp.dma_start(WM[u], wm[:, :, 512 * u:512 * (u + 1)]).then_inc(S(f"wmod_loaded{u}"), 16)
                        continue
                    lo = 0 if l else 1
                    with sp.Fori(lo, 4) as i:
                        for u in range(3):
                            sp.wait_ge(S("wmod_used"), 12 * l + i * 3 + (u - 2))
                            sp.dma_start(WM[u], wm[:, :, ds(i * 1536 + 512 * u, 512)]).then_inc(S(f"wmod_loaded{u}"), 16)

            def head_weights(ph, src, parts, cols):
                with sp.Fori(0, ph.iters // 2) as i2:
                    for b in range(2):
                        i = i2 * 2 + b
                        ph.wait(sp, "w_free", i + 1)
                        for dst, width, start, step in parts:
                            sp.dma_start(WC[b][:, :, dst:dst + width], src[:, :, ds(start + i * step, width)]
                                         ).then_inc(ph.s(f"w_loaded{b}"), 16)

            def w_out(l, src):
                wait(sp, "wo_free", l, 1)
                for n in range(2):
                    sp.dma_start(WO[n], src[:, :, 512 * n:512 * (n + 1)]).then_inc(S("wo_loaded"), 16)

            def experts(l):
                w1 = A["w1"][l].rearrange("e (k p) f -> e p k f", p=P)
                w3 = A["w3"][l].rearrange("e (k p) f -> e p k f", p=P)
                w2 = A["w2"][l].rearrange("e (k p) f -> e p k f", p=P)

                def load(e, u, up, down):
                    sp.dma_start(W1[u], w1[e]).then_inc(up, 16)
                    sp.dma_start(W3[u], w3[e]).then_inc(up, 16)
                    return down
                with sp.Fori(0, NE // 2) as i:
                    for u in range(2):
                        e = i * 2 + u
                        wait(sp, "up_free", l, e + 1)
                        sp.dma_start(W1[u], w1[ds(e, 1)].rearrange("e p k f -> (e p) k f")).then_inc(S(f"up_loaded{u}"), 16)
                        sp.dma_start(W3[u], w3[ds(e, 1)].rearrange("e p k f -> (e p) k f")).then_inc(S(f"up_loaded{u}"), 16)
                        wait(sp, "down_free", l, e + 1)
                        sp.dma_start(W2[u], w2[ds(e, 1)].rearrange("e p k f -> (e p) k f")).then_inc(S(f"down_loaded{u}"), 16)
                def block_weights(b, q):
                    ex = sp.value_load(OVI[0:1, l, ds(b, 1)], min_val=0, max_val=NE - 1)
                    sp.wait_ge(S("over_free"), q + 1 + l)
                    sp.dma_start(W1[0], w1[ds(ex, 1)].rearrange("e p k f -> (e p) k f")).then_inc(S("over_loaded"), 16)
                    sp.dma_start(W3[0], w3[ds(ex, 1)].rearrange("e p k f -> (e p) k f")).then_inc(S("over_loaded"), 16)
                    sp.dma_start(W2[0], w2[ds(ex, 1)].rearrange("e p k f -> (e p) k f")).then_inc(S("over_loaded"), 16)
                overflow(sp, l, block_weights)

                wait(sp, "y_all", l, 1)
                yt = y_d[l].rearrange("(t p k) d -> t p k d", p=P, k=2)
                for n, t in enumerate(tiles_of[l]):
                    if n >= 2:
                        wait(sp, "yg_used", l, n - 1)
                    sp.dma_start(YG[n % 2], yt[n]).then_inc(S(f"yg{n % 2}"), 16)

            we = A["w_in_even"][0].rearrange("(k p) n -> p k n", p=P)
            wd = A["w_in_odd"][0].rearrange("(k p) n -> p k n", p=P)
            head_weights(PA, we, [(0, 128, 0, 128), (128, 128, 512, 128), (256, 128, 1024, 128)], 384)
            sp.wait_ge(S("a0_w_free"), 6)
            sp.dma_start(WC[0][:, :, 0:256], we[:, :, 2048:2304]).then_inc(S("kv_loaded"), 16)
            head_weights(PBB, we, [(0, 64, 1536, 64), (64, 64, 1792, 64)], 128)
            w_out(0, A["w_out_even"][0].rearrange("(k p) n -> p k n", p=P))
            experts(0)
            head_weights(PN, wd, [(0, 128, 0, 128), (128, 128, 1024, 128), (256, 128, 2048, 128)], 384)
            w_out(1, A["w_out_odd"][0].rearrange("(k p) n -> p k n", p=P))
            experts(1)

            for n, t in enumerate(tiles_of[1]):
                wait(sp, "x_new", 1, n + 1)
                sp.dma_start(out[0, P * n:P * (n + 1), :], X[:, t, :]).then_inc(S("stored"), 16)
            sp.wait_ge(S("stored"), 16 * 4)

        @block.tensor
        def _(pe):
            mm = nc.tensor.matmul
            tr = nc.tensor.transpose
            pe.wait_ge(S("const_loaded"), 16)
            pe.wait_ge(S("c_loaded"), 32)
            tr(PB[:, 7, 0:2 * KT], CROW, ident[0:2 * KT, 0:2 * KT]).then_inc(S("c_T"), 1)
            pe.wait_ge(S("silu_c"), 1)
            for l in range(DEPTH):
                with pe.Fori(0, 4) as i:
                    for u in range(3):
                        pe.wait_ge(S(f"wmod_loaded{u}"), (i + 1 + 4 * l) * 16)
                        pe.wait_ge(S("mod_added"), 12 * l + i * 3 + (u + 1))
                        for k in range(KT):
                            last = mm(PB[0:2, u, :], SC[:, k, :], WM[u][:, k, :], start=k == 0, stop=k == KT - 1)
                        last.then_inc(S("wmod_used"), 1)
            for l in range(DEPTH):
                pe.wait_ge(S("mod_rows"), 2 * (l + 1))
                for j in range(48):
                    last = tr(PB[:, 4 + l, 2 * j:2 * j + 2], BM[l][:, P * j:P * (j + 1)], ident[0:2, 0:2])
                last.then_inc(S("mod_T"), 1)

            def stage_a(l):
                for n, t in enumerate(range(NT)):
                    if l == 0:
                        pe.wait_ge(S("ctx_loaded" if t < NCT else "x_loaded"), 16)
                    else:
                        pe.wait_ge(S("x_new"), n + 1)
                    if n >= 2:
                        wait(pe, "hTa", l, n - 1)
                        wait(pe, "hTd", l, n - 1)
                    for k in range(KT):
                        last = tr(PB[:, 2 * (n % 2) + k // 4, P * (k % 4):P * (k % 4 + 1)], X[:, t, P * k:P * (k + 1)], ident)
                    last.then_inc(S("xT"), 1)
                wait(pe, "hTa", l, NT)
                wait(pe, "hTd", l, NT)

            def project_rows(ph, i, w, width, trs):
                def mms(t):
                    if t >= 2:
                        ph.wait(pe, "pj_out", 6 * i + t - 1)
                    for k in range(KT):
                        last = mm(PB[:, 6 + t % 2, 0:width], HT[:, k, P * t:P * (t + 1)], w[:, k, 0:width],
                                  start=k == 0, stop=k == KT - 1)
                    last.then_inc(ph.s("pj"), 1)

                def trans(t):
                    ph.wait(pe, "rope", 6 * i + t + 1)
                    if t >= 2:
                        ph.wait(pe, "qk_out", 6 * i + t - 1)
                    for n in range(trs):
                        last = tr(PB[:, 4 + t % 2, P * n:P * (n + 1)], RO[:, t % 2, P * n:P * (n + 1)], ident)
                    last.then_inc(ph.s("qk_T"), 1)
                for t in range(NT):
                    mms(t)
                    if t:
                        trans(t - 1)
                trans(NT - 1)

            def attention(ph, i, kt, v):
                def scores(u):
                    t, s = ph.units[u]
                    if ph.maps == 2 and u >= 1:
                        ph.wait(pe, "exp", (ph.nu * i + u) * 2)
                    if ph.maps == 1 and u >= 2:
                        ph.wait(pe, "exp", ph.nu * i + u - 1)
                    for m in range(ph.maps):
                        r = ph.region(u, m)
                        qt = QT[:, m if ph.maps == 2 else s, P * (t - (NCT if ph.local else 0)):][:, 0:P]
                        if ph.local:
                            mm(PB[:, r, 0:512], qt, kt[:, CTX:NTOK], start=True, stop=True)
                            last = mm(PB[:, r + 1, 0:256], qt, kt[:, 0:CTX], start=True, stop=True)
                        elif t < NCT:
                            last = mm(PB[:, r, 0:256], qt, kt[:, 0:CTX], start=True, stop=True)
                        else:
                            mm(PB[:, r, 0:512], qt, kt[:, 0:512], start=True, stop=True)
                            last = mm(PB[:, r + 1, 0:256], qt, kt[:, 512:NTOK], start=True, stop=True)
                        last.then_inc(ph.s("scores"), 1)

                def trans(u):
                    t, s = ph.units[u]
                    g = ph.nu * i + u
                    ph.wait(pe, "probs" if ph.maps == 2 else "exp", g + 1)
                    if u >= 1:
                        ph.wait(pe, "pt_a", g)
                        ph.wait(pe, "pt_d", g)
                    js, n0 = ph.jt(t)
                    src = PR[:, u % 2, 0, :] if ph.maps == 2 else PR1[:, u % 2, :]
                    for j in range(len(js)):
                        b, c = (4, j) if j < n0 else (5, j - n0)
                        last = tr(PB[:, b, P * c:P * (c + 1)], src[:, P * j:P * (j + 1)], ident)
                    last.then_inc(ph.s("probs_T"), 1)

                def values(u):
                    t, s = ph.units[u]
                    g = ph.nu * i + u
                    ph.wait(pe, "pt_a", g + 1)
                    ph.wait(pe, "pt_d", g + 1)
                    if u >= 2:
                        ph.wait(pe, "o_out", g - 1)
                    js, n0 = ph.jt(t)
                    for j, kt_ in enumerate(js):
                        last = mm(PB[:, 6 + u % 2, 0:P], PT[:, u % 2, j, :], v[:, kt_, :],
                                  start=j == 0, stop=j == len(js) - 1)
                    last.then_inc(ph.s("o"), 1)

                scores(0)
                for u in range(ph.nu):
                    if u + 1 < ph.nu:
                        scores(u + 1)
                    trans(u)
                    if u:
                        values(u - 1)
                values(ph.nu - 1)
                ph.wait(pe, "o_out", ph.nu * (i + 1))

            def loop(ph, body):
                for _ in range(2):
                    pe.nop(nofuse=True).then_inc(ph.s("w_free"), 1)
                with pe.Fori(0, ph.iters // 2) as i2:
                    for b in range(2):
                        body(i2 * 2 + b, i2, b)

            def rows_iter(ph, width, trs, nw, kt, v):
                def body(i, i2, b):
                    ph.wait(pe, f"w_loaded{b}", (i2 + 1) * 16 * nw)
                    project_rows(ph, i, WC[b], width, trs)
                    ph.wait(pe, "qk_out", 6 * (i + 1))
                    pe.nop(nofuse=True).then_inc(ph.s("w_free"), 1)
                    attention(ph, i, kt, v)
                return body

            def odd_iter(i, i2, b):
                ph = PN
                ph.wait(pe, f"w_loaded{b}", (i2 + 1) * 48)
                w = WC[b]
                for k in range(KT):
                    last = mm(PB[:, 0, 0:512], w[:, k, 0:P], HT[:, k, CTX:NTOK], start=k == 0, stop=k == KT - 1)
                last.then_inc(ph.s("pq"), 1)
                for k in range(KT):
                    last = mm(PB[:, 1, 0:512], w[:, k, P:2 * P], HT[:, k, 0:512], start=k == 0, stop=k == KT - 1)
                last.then_inc(ph.s("pq"), 1)
                for k in range(KT):
                    last = mm(PB[:, 2, 0:256], w[:, k, P:2 * P], HT[:, k, 512:NTOK], start=k == 0, stop=k == KT - 1)
                last.then_inc(ph.s("pq"), 1)
                for t in range(NT):
                    bank, c = (6, t) if t < 4 else (7, t - 4)
                    for k in range(KT):
                        last = mm(PB[:, bank, P * c:P * (c + 1)], HT[:, k, P * t:P * (t + 1)], w[:, k, 2 * P:3 * P],
                                  start=k == 0, stop=k == KT - 1)
                    if t in (3, 5):
                        last.then_inc(ph.s("pq"), 1)
                ph.wait(pe, "qkv_out", 5 * (i + 1))
                pe.nop(nofuse=True).then_inc(ph.s("w_free"), 1)
                attention(ph, i, KTr, V)

            def stage_c(l):
                tl = tiles_of[l]
                n_t = len(tl)
                nth = [0]

                def bank45(src, ready):
                    ready()
                    if nth[0]:
                        wait(pe, "cTa", l, nth[0])
                        wait(pe, "cTd", l, nth[0])
                    for k in range(KT):
                        last = tr(PB[:, 4 + k // 4, P * (k % 4):P * (k % 4 + 1)], src[:, P * k:P * (k + 1)], ident)
                    last.then_inc(S("cT"), 1)
                    nth[0] += 1
                    return nth[0]

                def o_t(n):
                    return bank45(OO[:, tl[n], :], (lambda: pe.wait_ge(S("o_normed"), n + 1)) if l == 0 else (lambda: None))

                def h_t(n):
                    return bank45(OO[:, tl[n], :], lambda: wait(pe, "h2", l, n + 1))

                def mix(n, done):
                    wait(pe, "cTa", l, done)
                    wait(pe, "cTd", l, done)
                    if n >= 2:
                        wait(pe, "mix_used", l, n - 1)
                    t = tl[n]
                    for h in range(2):
                        for k in range(KT):
                            last = mm(PB[:, 2 * (n % 2) + h, 0:512], HT[:, k, P * t:P * (t + 1)], WO[h][:, k, :],
                                      start=k == 0, stop=k == KT - 1)
                    last.then_inc(S("mix"), 1)

                def route(n, done):
                    wait(pe, "cTa", l, done)
                    wait(pe, "cTd", l, done)
                    if n >= 2:
                        wait(pe, "lg_out", l, n - 1)
                    for k in range(KT):
                        last = mm(PB[:, 6 + n % 2, 0:NG + NE], H2T[:, n % 2, k, :], RW[:, k, :], start=k == 0, stop=k == KT - 1)
                    last.then_inc(S("lg"), 1)

                pe.nop(nofuse=True).then_inc(S("wo_free"), 1)
                o_done = {0: o_t(0)}
                wait(pe, "wo_loaded", l, 32)
                wait(pe, "rw_loaded", l, 32)
                h_done = {}
                for n in range(n_t + 2):
                    if n < n_t:
                        if n + 1 < n_t:
                            o_done[n + 1] = o_t(n + 1)
                        mix(n, o_done[n])
                    if 1 <= n <= n_t:
                        h_done[n - 1] = h_t(n - 1)
                    if n == n_t:
                        pe.nop(nofuse=True).then_inc(S("up_free"), 1)
                    if n >= 2:
                        route(n - 2, h_done[n - 2])
                wait(pe, "lg_out", l, n_t)
                pe.nop(nofuse=True).then_inc(S("down_free"), 1)

            def ranks(l):
                tl = MOE_TILES[l]
                wait(pe, "chosen", l, 1)
                for n in range(len(tl)):
                    for n2 in range(n):
                        mm(PB[:, 6, NE * n:NE * (n + 1)], ones, grid(2)[:, n2, :], start=n2 == 0, stop=False)
                    mm(PB[:, 6, NE * n:NE * (n + 1)], tri, grid(2)[:, n, :], start=n == 0, stop=True)
                for n in range(len(tl)):
                    last = mm(PB[:, 6, 256:256 + NE], ones, grid(2)[:, n, :], start=n == 0, stop=n == len(tl) - 1)
                last.then_inc(S("ranks"), 1)

            def experts(l):
                def x_t(e, u):
                    wait(pe, f"xg{u}", l, (e + 2 - u) * 8)
                    for k in range(KT):
                        last = tr(PB[:, 4 + k // 4, P * (k % 4):P * (k % 4) + CAP], XG[u][0:CAP, P * k:P * (k + 1)],
                                  ident[0:CAP, 0:CAP])
                    last.then_inc(S("xgT"), 1)

                def up(e, u, xt_a, xt_d, loaded, free):
                    loaded()
                    wait(pe, xt_a, l, e + 1)
                    wait(pe, xt_d, l, e + 1)
                    for w, (W, bank) in enumerate(((W1[u], 0), (W3[u], 1))):
                        for f in range(4):
                            for k in range(KT):
                                last = mm(PB[:, 2 * u + bank, CAP * f:CAP * (f + 1)], W[:, k, P * f:P * (f + 1)],
                                          XT[u][:, k, 0:CAP], start=k == 0, stop=k == KT - 1)
                        last.then_inc(S(free[w]), 1)

                def down(e, u, hx, loaded, out_a, out_d, done):
                    wait(pe, hx, l, e + 1)
                    loaded()
                    if out_a is not None:
                        wait(pe, out_a, l, e)
                        wait(pe, out_d, l, e)
                    for h in range(2):
                        for f in range(4):
                            last = mm(PB[0:CAP, 6 + h, 0:512], HX[u][:, f, 0:CAP], W2[u][:, f, 512 * h:512 * (h + 1)],
                                      start=f == 0, stop=f == 3)
                    last.then_inc(S(done), 1)

                def main_up(e, u):
                    up(e, u, "xTa", "xTd", lambda: wait(pe, f"up_loaded{u}", l, (e + 2 - u) * 16),
                       ("up1", "up_free"))

                def main_down(e, u):
                    down(e, u, "hx", lambda: wait(pe, f"down_loaded{u}", l, (e + 2 - u) * 8),
                         "y_a", "y_d", "down_free")

                x_t(0, 0)
                wait(pe, "xTa", l, 1)
                wait(pe, "xTd", l, 1)
                x_t(1, 1)
                main_up(0, 0)
                with pe.Fori(0, NE // 2 - 1) as i:
                    for u in (1, 0):
                        e = i * 2 + (1 if u else 2)
                        wait(pe, "xTa", l, e + 1)
                        wait(pe, "xTd", l, e + 1)
                        x_t(e + 1, 1 - u)
                        main_up(e, u)
                        main_down(e - 1, 1 - u)
                main_up(NE - 1, 1)
                main_down(NE - 2, 0)
                main_down(NE - 1, 1)

                wait(pe, "y_a", l, NE)
                wait(pe, "y_d", l, NE)
                pe.nop(nofuse=True).then_inc(S("over_free"), 1)

                def over_block(b, q):
                    pe.wait_ge(S("over_xg"), (q + 1) * 16)
                    for k in range(KT):
                        last = tr(PB[:, 4 + k // 4, P * (k % 4):P * (k % 4) + CAP], XG[0][0:CAP, P * k:P * (k + 1)],
                                  ident[0:CAP, 0:CAP])
                    last.then_inc(S("over_xgT"), 1)
                    up(q, 0, "over_xTa", "over_xTd", lambda: pe.wait_ge(S("over_loaded"), (q + 1) * 48), ("over_up1", "over_up"))
                    down(q, 0, "over_hx", lambda: None, None, None, "over_free")
                overflow(pe, l, over_block)

            pe.wait_ge(S("mod_ready"), 2)
            stage_a(0)
            loop(PA, rows_iter(PA, 384, 2, 3, KTr, V))
            pe.wait_ge(S("kv_loaded"), 16)
            project_rows(Phase("kv", 1, [], 1, False), 0, WC[0], 256, 1)
            pe.wait_ge(S("kv_qk_out"), 6)
            loop(PBB, rows_iter(PBB, 128, 1, 2, BK, BV))
            for name in ("up_free", "down_free"):
                pe.nop(nofuse=True).then_inc(S(name), 1)
            stage_c(0)
            ranks(0)
            experts(0)
            stage_a(1)
            loop(PN, odd_iter)
            for name in ("up_free", "down_free"):
                pe.nop(nofuse=True).then_inc(S(name), 1)
            stage_c(1)
            ranks(1)
            experts(1)

        @block.scalar
        def _(act):
            fn = nc.scalar.activation
            act.nop(nofuse=True).then_inc(S("y_a"), CREDIT["y_a"])
            act.dma_start(CO[:, :], A["consts"]).then_inc(S("const_loaded"), 16)
            act.dma_start(CROW[0:KT, :], A["c"].rearrange("o (k p) -> (o k) p", p=P)).then_inc(S("c_loaded"), 16)
            act.dma_start(CROW[KT:2 * KT, :], A["c_ctx"].rearrange("(k p) -> k p", p=P)).then_inc(S("c_loaded"), 16)
            for l in range(DEPTH):
                act.dma_start(BM[l], A["b_mod"][l].partition_broadcast(2)).then_inc(S("bmod_loaded"), 16)
            act.dma_start(X[:, 0:NCT, :], A["ctx"][0].rearrange("(t p) d -> p t d", p=P)).then_inc(S("ctx_loaded"), 16)
            act.dma_start(X[:, NCT:NT, :], A["x"][0].rearrange("(t p) d -> p t d", p=P)).then_inc(S("x_loaded"), 16)
            act.dma_start(TAB[:, 0, :, :, :], A["rope"]).then_inc(S("rope_loaded"), 16)
            act.dma_start(QG[:, :, :].rearrange("p a n -> p (a n)"), A["gqa_qk_g"][0].rearrange("a n -> (a n)").partition_broadcast(P)).then_inc(S("small_loaded"), 16)
            act.dma_start(SUBG[:, :], A["diff_subln_g"][0].partition_broadcast(P)).then_inc(S("small_loaded"), 16)
            act.dma_start(LMV[:, :, :].rearrange("p a n -> p (a n)"), A["diff_lam"][0].rearrange("a n -> (a n)").partition_broadcast(P)).then_inc(S("small_loaded"), 16)

            act.wait_ge(S("c_T"), 1)
            fn(SC[:, :, :], PB[:, 7, 0:2 * KT].rearrange("p (m k) -> p k m", m=2), ACT.Silu).then_inc(S("silu_c"), 1)
            act.wait_ge(S("lam_dots"), 1)
            fn(LAM[:, 0:2], LAM[:, 0:2], ACT.Exp).then_inc(S("lam_exp"), 1)
            for l in range(DEPTH):
                act.wait_ge(S("mod_rows"), 2 * (l + 1))
                act.dma_start(mod_d[l].rearrange("(m j) p -> m (j p)", m=2), BM[l]).then_inc(S("mod_stored"), 16)
            act.wait_ge(S("mod_ready"), 2)
            act.wait_ge(S("mod_stored"), 32)

            def rows_c(l):
                for m in range(2):
                    act.dma_start(ROWS[:, ROW_G + m, :], mod_row(l, 2, m)).then_inc(S("rows"), 16)
                    act.dma_start(ROWS[:, ROW_SC + m, :], mod_row(l, 4, m)).then_inc(S("rows"), 16)
                    act.dma_start(ROWS[:, ROW_SH + m, :], mod_row(l, 3, m)).then_inc(S("rows"), 16)
                act.dma_start(ROWS[:, ROW_LG, :], A["ln_g"][l, 0].partition_broadcast(P)).then_inc(S("rows"), 16)
                act.dma_start(ROWS[:, ROW_LB, :], A["ln_b"][l, 0].partition_broadcast(P)).then_inc(S("rows"), 16)
                act.dma_start(RW[:, :, 0:NG], A["router_g"][l].rearrange("(k p) n -> p k n", p=P)).then_inc(S("rw_loaded"), 16)
                act.dma_start(RW[:, :, NG:NG + NE], A["router_e"][l].rearrange("(k p) n -> p k n", p=P)).then_inc(S("rw_loaded"), 16)

            def rows_f(l):
                for m in range(2):
                    act.dma_start(ROWS[:, ROW_G + m, :], mod_row(l, 5, m)).then_inc(S("rowsf"), 16)
                act.dma_start(ROWS[:, ROW_LG, :], A["ln_g"][l, 1].partition_broadcast(P)).then_inc(S("rowsf"), 16)
                act.dma_start(ROWS[:, ROW_LB, :], A["ln_b"][l, 1].partition_broadcast(P)).then_inc(S("rowsf"), 16)

            def stage_a(l):
                for n, t in enumerate(range(NT)):
                    m = m_of(t)
                    wait(act, "xT", l, n + 1)
                    for k in range(4):
                        last = fn(HT[:, k, P * t:P * (t + 1)], PB[:, 2 * (n % 2), P * k:P * (k + 1)], ACT.Identity,
                                  bias=MT[:, l, m, k:k + 1], scale=MT[:, l, m, 8 + k:9 + k])
                    last.then_inc(S("hTa"), 1)

            def project_rows(ph, i, wqk, vdst, kdst, qdst, b0):
                def take(t):
                    ph.wait(act, "pj", 6 * i + t + 1)
                    if t >= 2:
                        ph.wait(act, "rope", 6 * i + t - 1)
                    if vdst is not None:
                        fn(vdst[:, t, :], PB[:, 6 + t % 2, wqk:wqk + P], ACT.Copy)
                    fn(RS[:, t % 2, 0:wqk], PB[:, 6 + t % 2, 0:wqk], ACT.Copy).then_inc(ph.s("pj_out"), 1)

                def give(t):
                    ph.wait(act, "qk_T", 6 * i + t + 1)
                    n = 0
                    if qdst is not None:
                        for s in range(2):
                            h = slice(HD * s, HD * (s + 1))
                            last = fn(qdst[h, s, P * t:P * (t + 1)], PB[h, 4 + t % 2, 0:P], ACT.Copy, scale=HD ** -0.5)
                        n = 1
                    if kdst is not None:
                        last = fn(kdst[:, P * t:P * (t + 1)], PB[:, 4 + t % 2, P * n:P * (n + 1)], ACT.Copy)
                    last.then_inc(ph.s("qk_out"), 1)
                for t in range(NT):
                    take(t)
                    if t:
                        give(t - 1)
                give(NT - 1)

            def attention(ph, i):
                def exps(u):
                    t, s = ph.units[u]
                    g = ph.nu * i + u
                    if u >= 2:
                        ph.wait(act, "probs_T", g - 1)
                    if u >= 4:
                        ph.wait(act, "o_out", g - 3)
                    for m in range(ph.maps):
                        r = ph.region(u, m)
                        ph.wait(act, "max", ph.maps * g + m + 1)
                        nm = NMX[:, u % 4, m:m + 1]
                        if ph.local:
                            fn(PR1[:, u % 2, 0:512], PR1[:, u % 2, 0:512], ACT.Exp, bias=nm, accum_out=SUM[:, u % 4, 0:1])
                            fn(PR1[:, u % 2, 512:768], PB[:, r + 1, 0:256], ACT.Exp, bias=nm,
                               accum_out=SUM[:, u % 4, 1:2]).then_inc(ph.s("exp"), 1)
                        else:
                            n = ph.nk(t)
                            dst = PR[:, u % 2, m, 0:n] if ph.maps == 2 else PR1[:, u % 2, 0:n]
                            fn(dst, PF[:, 512 * r:512 * r + n], ACT.Exp, bias=nm,
                               accum_out=SUM[:, u % 4, m:m + 1]).then_inc(ph.s("exp"), 1)

                def take(u):
                    t, s = ph.units[u]
                    g = ph.nu * i + u
                    js, n0 = ph.jt(t)
                    ph.wait(act, "probs_T", g + 1)
                    if u >= 2:
                        ph.wait(act, "o", g - 1)
                    fn(PT[:, u % 2, 0:n0, :], PB[:, 4, 0:P * n0].rearrange("p (j n) -> p j n", j=n0), ACT.Copy
                       ).then_inc(ph.s("pt_a"), 1)
                exps(0)
                for u in range(ph.nu):
                    if u + 1 < ph.nu:
                        exps(u + 1)
                    take(u)

            def stage_c(l):
                tl = tiles_of[l]
                n_t = len(tl)
                cnt = [0]

                def o_t(n):
                    cnt[0] += 1
                    wait(act, "cT", l, cnt[0])
                    t = tl[n]
                    fn(HT[:, 0:4, P * t:P * (t + 1)], PB[:, 4, :].rearrange("p (k n) -> p k n", k=4), ACT.Copy).then_inc(S("cTa"), 1)

                def h_t(n):
                    cnt[0] += 1
                    wait(act, "cT", l, cnt[0])
                    if n >= 2:
                        wait(act, "lg", l, n - 1)
                    fn(H2T[:, n % 2, 0:4, :], PB[:, 4, :].rearrange("p (k n) -> p k n", k=4), ACT.Copy).then_inc(S("cTa"), 1)

                o_t(0)
                for n in range(n_t + 2):
                    if n + 1 < n_t:
                        o_t(n + 1)
                    if 1 <= n <= n_t:
                        wait(act, "h2", l, n)
                        act.dma_start(h2_d[l][P * (n - 1):P * n, :], OO[:, tl[n - 1], :]).then_inc(S("h2_stored"), 16)
                        h_t(n - 1)
                    if n >= 2:
                        wait(act, "lg", l, n - 1)
                        fn(LG[:, n - 2, :], PB[:, 6 + n % 2, 0:NG + NE], ACT.Copy).then_inc(S("lg_out"), 1)

            def routing(l):
                wait(act, "gmax", l, 1)
                n = len(MOE_TILES[l])
                fn(grid(6, NG)[:, 0:n, :], grid(6, NG)[:, 0:n, :], ACT.Exp).then_inc(S("gexp"), 1)
                wait(act, "top2", l, 1)
                fn(GATE[:, 1, 0:n], GATE[:, 1, 0:n], ACT.Exp).then_inc(S("texp"), 1)

            def experts(l):
                def x_t(e, u, s_t, s_out):
                    wait(act, s_t, l, e + 1)
                    fn(XT[u][:, 0:4, 0:CAP], PB[:, 4, :].rearrange("p (k n) -> p k n", k=4)[:, :, 0:CAP], ACT.Copy).then_inc(S(s_out), 1)

                def gate(e, u, s_up, s_sg):
                    wait(act, s_up, l, e + 1)
                    fn(SG[u], PB[:, 2 * u, 0:4 * CAP].rearrange("p (f n) -> p f n", f=4), ACT.Silu).then_inc(S(s_sg), 1)

                def y_out(e, u, s_down, base, s_out):
                    wait(act, s_down, l, base + e + 1)
                    fn(YS[u][0:CAP, 0:512], PB[0:CAP, 6, 0:512], ACT.Copy).then_inc(S(s_out), 1)

                def main_y(e, u, first=False):
                    if not first:
                        wait(act, f"y_stored{u}", l, (e - u) * 8)
                    y_out(e, u, "down_free", 2, "y_a")

                s_t, s_o, s_u, s_g = "xgT", "xTa", "up1", "sg"
                x_t(0, 0, s_t, s_o)
                x_t(1, 1, s_t, s_o)
                gate(0, 0, s_u, s_g)
                x_t(2, 0, s_t, s_o)
                gate(1, 1, s_u, s_g)
                main_y(0, 0, True)
                x_t(3, 1, s_t, s_o)
                gate(2, 0, s_u, s_g)
                main_y(1, 1, True)
                with act.Fori(1, NE // 2 - 1) as i:
                    for u in (1, 0):
                        e = i * 2 + (1 if u else 2)
                        x_t(e + 1, 1 - u, s_t, s_o)
                        gate(e, u, s_u, s_g)
                        main_y(e - 1, 1 - u)
                gate(NE - 1, 1, s_u, s_g)
                main_y(NE - 2, 0)
                main_y(NE - 1, 1)
                for u in range(2):
                    wait(act, f"y_stored{u}", l, NE * 8)

                def over_block(b, q):
                    x_t(q, 0, "over_xgT", "over_xTa")
                    gate(q, 0, "over_up1", "over_sg")
                    y_out(q, 0, "over_free", 1 + l, "over_ya")
                    lone_wait(act, S("over_block"), q + 1)
                overflow(act, l, over_block)

            rows_c(0)
            stage_a(0)

            def half(ph, body):
                with act.Fori(0, ph.iters) as i:
                    body(i)

            half(PA, lambda i: (project_rows(PA, i, 256, V, KTr, QT, 0), attention(PA, i)))
            project_rows(Phase("kv", 1, [], 1, False), 0, 128, BV, BK, None, 0)
            half(PBB, lambda i: (project_rows(PBB, i, 128, None, None, QT, 0), attention(PBB, i)))
            stage_c(0)
            act.wait_ge(S("h2"), NT)
            rows_f(0)
            routing(0)
            experts(0)
            act.wait_ge(S("x_new"), NT)
            rows_c(1)
            stage_a(1)

            def odd(i):
                ph = PN
                ph.wait(act, "pq", 5 * i + 1)
                fn(QT[0:HD, 0, 0:512], PB[0:HD, 0, :], ACT.Copy, scale=HD ** -0.5)
                fn(QT[HD:P, 1, 0:512], PB[HD:P, 0, :], ACT.Copy, scale=HD ** -0.5).then_inc(ph.s("qkv_out"), 1)
                ph.wait(act, "pq", 5 * i + 2)
                fn(KTr[:, 0:512], PB[:, 1, :], ACT.Copy).then_inc(ph.s("qkv_out"), 1)
                ph.wait(act, "pq", 5 * i + 3)
                fn(KTr[:, 512:768], PB[:, 2, 0:256], ACT.Copy).then_inc(ph.s("qkv_out"), 1)
                ph.wait(act, "pq", 5 * i + 4)
                fn(V[:, 0:4, :], PB[:, 6, :].rearrange("p (t n) -> p t n", t=4), ACT.Copy).then_inc(ph.s("qkv_out"), 1)
                ph.wait(act, "pq", 5 * i + 5)
                fn(V[:, 4:6, :], PB[:, 7, 0:256].rearrange("p (t n) -> p t n", t=2), ACT.Copy).then_inc(ph.s("qkv_out"), 1)
                attention(ph, i)
            half(PN, odd)
            stage_c(1)
            wait(act, "h2", 1, 4)
            rows_f(1)
            routing(1)
            experts(1)

        @block.gpsimd
        def _(po):
            tt = nc.gpsimd.tensor_tensor
            nc.gpsimd.memset(MHALF[:, :], -0.5).then_inc(S("mhalf"), 1)
            nc.gpsimd.memset(IDX[:, :], EMPTY).then_inc(S("idx_zero"), 1)
            po.wait_ge(S("mod_ready"), 2)
            po.dma_start(skew_d.rearrange("(c n) -> c n", n=LR),
                         A["na_rpb"].rearrange("o h a b -> o (h a b)")[0].partition_broadcast(GRID_W)).then_inc(S("skewed"), 16)
            po.wait_ge(S("idx_zero"), 1)
            for l in range(DEPTH):
                po.dma_start(tab_d[l].rearrange("(r b) o -> r (b o)", b=NB), IDX[0:CAP, :]).then_inc(S("tab_zero"), 16)
            po.wait_ge(S("tab_zero"), 32)
            po.wait_ge(S("mhalf"), 1)

            def root(what, n, lo, hi, src):
                po.wait_ge(S(f"{what}_ms"), n)
                tt(src[:, lo:hi], src[:, lo:hi], MHALF[:, 0:hi - lo], ALU.pow).then_inc(S(f"{what}_root"), 1)

            def roots(what, count):
                with po.Fori(0, count) as n:
                    root(what, n + 1, 0, 2, MS)
            roots("kv", NT)
            roots("b0", 4 * NT)

            def layer(l):
                tl = tiles_of[l]
                if l == 0:
                    root("sub", 1, 0, 4, MS)
                for n in range(len(tl)):
                    if l == 0 and n + 1 < NT:
                        root("sub", n + 2, 0, 4, MS)
                    root("ln", n + 1 + l * NT, 1, 2, MV)
                wait(po, "routed", l, 1)
                for k in range(2):
                    for n in range(len(tl)):
                        po.indirect_dma_start(tab_d[l], bass.IndirectOffsetOnAxis(ap=ADI[:, k, n:n + 1], axis=0),
                                              TOKI[:, k, n:n + 1], None).then_inc(S("scattered"), 16)
                wait(po, "scattered", l, 32 * len(tl))
                po.dma_start(IDX[0:CAP, :], tab_d[l].rearrange("(r b) o -> r (b o)", b=NB)).then_inc(S("slots"), 16)
                wait(po, "h2_stored", l, 16 * len(tl))
                wait(po, "tokens", l, 1)

                def gather(col, u, s_ix, n_ix, s_x):
                    nc.gpsimd.tensor_copy(IX[0:CAP, u:u + 1], IDT[0:CAP, ds(col, 1)]).then_inc(S(s_ix), 1)
                    lone_wait(po, S(s_ix), n_ix + l * LAYER0.get(s_ix, 0))
                    po.indirect_dma_start(XG[u][0:CAP, :], None, h2_d[l], bass.IndirectOffsetOnAxis(ap=IX[0:CAP, u:u + 1], axis=0),
                                          bounds_check=MOE_TOK[l] - 1, oob_is_err=False).then_inc(S(s_x), 16)

                def scatter(col, u, s_iy, n_iy, s_y):
                    nc.gpsimd.tensor_copy(IY[0:CAP, u:u + 1], IDX[0:CAP, ds(col, 1)]).then_inc(S(s_iy), 1)
                    lone_wait(po, S(s_iy), n_iy + l * LAYER0.get(s_iy, 0))
                    po.indirect_dma_start(y_d[l], bass.IndirectOffsetOnAxis(ap=IY[0:CAP, u:u + 1], axis=0), YS[u][0:CAP, :], None,
                                          bounds_check=2 * MOE_TOK[l] - 1, oob_is_err=False).then_inc(S(s_y), 16)

                def main_scatter(e, u):
                    wait(po, "y_a", l, e + 1)
                    wait(po, "y_d", l, e + 1)
                    scatter(e, u, "iy", e + 1, f"y_stored{u}")
                for e in range(4):
                    if e >= 2:
                        wait(po, "xgT", l, e - 1)
                    gather(e, e % 2, "ix", e + 1, f"xg{e % 2}")
                with po.Fori(2, NE // 2) as i:
                    for u in range(2):
                        e = i * 2 + u
                        wait(po, "xgT", l, e - 1)
                        gather(e, u, "ix", e + 1, f"xg{u}")
                        main_scatter(e - 4, u)
                for e in range(NE - 4, NE):
                    main_scatter(e, e % 2)
                wait(po, "xgT", l, NE)
                for u in range(2):
                    wait(po, f"y_stored{u}", l, NE * 8)

                def over_block(b, q):
                    po.wait_ge(S("over_free"), q + 1 + l)
                    gather(b + NE, 0, "over_ix", q + 1, "over_xg")
                    po.wait_ge(S("over_ya"), q + 1)
                    po.wait_ge(S("over_yd"), q + 1)
                    scatter(b + NE, 0, "over_iy", q + 1, "over_stored")
                    po.wait_ge(S("over_stored"), (q + 1) * 16)
                    po.nop(nofuse=True).then_inc(S("over_block"), 1)
                overflow(po, l, over_block)
                po.nop(nofuse=True).then_inc(S("y_all"), 1)
                for n in range(len(tl)):
                    root("lnf", n + 1 + l * NT, 1, 2, MV)

            layer(0)

            po.wait_ge(S("skewed"), 16)
            with po.Fori(0, PN.iters) as i:
                po.wait_ge(S("n1_w_free"), i + 2)
                po.wait_ge(PN.s("max"), i * PN.nu + PN.before["max"])
                for r2 in range(2):
                    src = bass.AP(skew_d.tensor, (1 - r2) * RPB_W + 15, [[LR - 1, GRID_W], [RPB_H * RPB_W, 16], [1, 467]])
                    po.dma_start(RAW[64 * r2:64 * (r2 + 1), :, 0:467], src[:, ds(i * 2, 2), :]).then_inc(S("raw"), 16)
                po.wait_ge(S("raw"), (i + 1) * 32)
                for s in range(2):
                    r = RAW[:, s, 0:467]
                    view = bass.AP(r.tensor, r.offset, [list(r.ap[0]), [RPB_W, 14], [1, GRID_W]])
                    tt(GT[:, s, :, :], view, colmask.unsqueeze(1).to_broadcast([P, 14, GRID_W]), ALU.add).then_inc(S("bias"), 1)
            layer(1)

        @block.vector
        def _(ve):
            v = nc.vector
            st = Steps(ve, S("dve_steps"))
            ve.nop(nofuse=True).then_inc(S("y_d"), CREDIT["y_d"])
            ve.nop(nofuse=True).then_inc(S("mod_added"), 3)
            ve.wait_ge(S("small_loaded"), 48)
            ve.wait_ge(S("const_loaded"), 16)
            st.did(v.tensor_copy(TOKI[:, 0, :], CO[:, C_TOK:C_TOK + NT]))
            st.did(v.tensor_scalar(TOKI[:, 1, :], CO[:, C_TOK:C_TOK + NT], 1.0, None, ALU.add))
            st.then(v.tensor_tensor(LMT[:, :, :], LMV[:, 0:4:2, :], LMV[:, 1:4:2, :], ALU.mult))
            v.tensor_reduce(LAM[:, 0:2], LMT[:, :, :], AX.X, ALU.add).then_inc(S("lam_dots"), 1)
            ve.wait_ge(S("lam_exp"), 1)
            st.then(v.tensor_tensor(LAM[:, 2:3], LAM[:, 1:2], LAM[:, 0:1], ALU.subtract))
            st.then(v.tensor_scalar(LAM[:, 3:4], LAM[:, 2:3], -LAM_INIT, None, ALU.add))
            st.did(v.tensor_scalar(SUBG[:, :], SUBG[:, :], 1.0 - LAM_INIT, None, ALU.mult))
            ve.wait_ge(S("rope_loaded"), 16)
            for a in range(2):
                g = QG[:, a, :]
                st.did(v.tensor_tensor(TAB[:, 1 + a, :, 0, :], TAB[:, 0, :, 0, :], g.unsqueeze(1).to_broadcast([P, NT, HD]), ALU.mult))
                for half in range(2):
                    gs = g.rearrange("p (b h n) -> p b h n", b=2, h=2)[:, :, 1 - half, :]
                    dst = TAB[:, 1 + a, :, 1, :].rearrange("p t (b h n) -> p t b h n", b=2, h=2)[:, :, :, half, :]
                    src = TAB[:, 0, :, 1, :].rearrange("p t (b h n) -> p t b h n", b=2, h=2)[:, :, :, half, :]
                    st.did(v.tensor_tensor(dst, src, gs.unsqueeze(1).to_broadcast([P, NT, 2, 16]), ALU.mult))
            st.settle()
            ve.wait_ge(S("bmod_loaded"), 32)
            for l in range(DEPTH):
                with ve.Fori(0, 4) as i:
                    for u in range(3):
                        part = BM[l][:, ds(i * 1536 + 512 * u, 512)]
                        ve.wait_ge(S("wmod_used"), 12 * l + i * 3 + (u + 1))
                        v.tensor_tensor(part, part, PB[0:2, u, :], ALU.add).then_inc(S("mod_added"), 1)
                ve.wait_ge(S("mod_added"), 3 + 12 * (l + 1))
                for a in (1, 4):
                    part = BM[l][:, D * a:D * (a + 1)]
                    v.tensor_scalar(part, part, 1.0, None, ALU.add).then_inc(S("mod_rows"), 1)
            for l in range(DEPTH):
                ve.wait_ge(S("mod_T"), l + 1)
                v.tensor_copy(MT[:, l, :, :], PB[:, 4 + l, 0:96].rearrange("p (j m) -> p m j", m=2)).then_inc(S("mod_ready"), 1)
            ve.wait_ge(S("mod_stored"), 32)
            ve.wait_ge(S("mod_ready"), 2)

            def stage_a(l):
                st.did(v.memset(QT[HD:P, 0, :], 0.0))
                st.then(v.memset(QT[0:HD, 1, :], 0.0))
                for n, t in enumerate(range(NT)):
                    m = m_of(t)
                    wait(ve, "xT", l, n + 1)
                    for k in range(4, 8):
                        last = v.tensor_scalar(HT[:, k, P * t:P * (t + 1)], PB[:, 2 * (n % 2) + 1, P * (k - 4):P * (k - 3)],
                                               MT[:, l, m, 8 + k:9 + k], MT[:, l, m, k:k + 1], ALU.mult, ALU.add)
                    last.then_inc(S("hTd"), 1)

            def rope(ph, i, t, tab, groups, norm):
                w = HD * groups
                if t:
                    ph.wait(ve, "rope", 6 * i + t)
                ph.wait(ve, "pj_out", 6 * i + t + 1)
                x = RS[:, t % 2, 0:w].rearrange("p (g n) -> p g n", g=groups)
                r1 = RT[:, 0, 0:w].rearrange("p (g n) -> p g n", g=groups)
                r2 = RT[:, 1, 0:w].rearrange("p (g n) -> p g n", g=groups)
                if norm:
                    st.then(v.tensor_tensor(r1, x, x, ALU.mult))
                    st.then(v.tensor_reduce(MS[:, 4:4 + groups], r1, AX.X, ALU.add))
                    v.tensor_scalar(MS[:, 0:groups], MS[:, 4:4 + groups], 1.0 / HD, EPS, ALU.mult, ALU.add).then_inc(ph.s("ms"), 1)
                st.did(v.tensor_tensor(r1, x, TAB[:, tab, t, 0, :].unsqueeze(1).to_broadcast([P, groups, HD]), ALU.mult))
                for half in range(2):
                    xs = x.rearrange("p g (b h n) -> p g b h n", b=2, h=2)[:, :, :, 1 - half, :]
                    sn = TAB[:, tab, t, 1, :].rearrange("p (b h n) -> p b h n", b=2, h=2)[:, :, half, :]
                    dst = r2.rearrange("p g (b h n) -> p g b h n", b=2, h=2)[:, :, :, half, :]
                    st.did(v.tensor_tensor(dst, xs, sn.unsqueeze(1).to_broadcast([P, groups, 2, 16]), ALU.mult))
                st.settle()
                if t >= 2:
                    ph.wait(ve, "qk_T", 6 * i + t - 1)
                dst = RO[:, t % 2, 0:w].rearrange("p (g n) -> p g n", g=groups)
                if norm:
                    st.then(v.tensor_tensor(r1, r1, r2, ALU.add))
                    ph.wait(ve, "root", 6 * i + t + 1)
                    v.tensor_tensor(dst, r1, MS[:, 0:groups].unsqueeze(2).to_broadcast([P, groups, HD]), ALU.mult).then_inc(ph.s("rope"), 1)
                else:
                    v.tensor_tensor(dst, r1, r2, ALU.add).then_inc(ph.s("rope"), 1)

            def attention(ph, i, col):
                def maxima(u):
                    t, s = ph.units[u]
                    g = ph.nu * i + u
                    if u >= 4:
                        ph.wait(ve, "max", ph.maps * (g - 3))
                    for m in range(ph.maps):
                        r = ph.region(u, m)
                        ph.wait(ve, "scores", ph.maps * g + m + 1)
                        if ph.local:
                            if u >= 2:
                                ph.wait(ve, "probs_T", g - 1)
                            st.did(v.tensor_reduce(RCP[:, u % 4, 2:3], PB[:, r + 1, 0:256], AX.X, ALU.max))
                            lone_wait(ve, st.sem, st.base + st.n)
                            n = t - NCT
                            v8 = lambda a: a.rearrange("p (j n) -> p j n", j=8)
                            st.then(v.tensor_tensor_reduce(out=v8(PR1[:, u % 2, 0:512]), in0=v8(PB[:, r, 0:512]),
                                                           in1=GT[:, s, 6 - 2 * n:14 - 2 * n, :], scale=1.0,
                                                           scalar=RCP[:, u % 4, 2:3], op0=ALU.add, op1=ALU.max,
                                                           accum_out=RCP[:, u % 4, 3:4]))
                            v.tensor_scalar(NMX[:, u % 4, 0:1], RCP[:, u % 4, 3:4], -1.0, None, ALU.mult).then_inc(ph.s("max"), 1)
                        else:
                            st.then(v.tensor_reduce(RCP[:, u % 4, 2 + m:3 + m], PF[:, 512 * r:512 * r + ph.nk(t)], AX.X, ALU.max))
                            v.tensor_scalar(NMX[:, u % 4, m:m + 1], RCP[:, u % 4, 2 + m:3 + m], -1.0, None, ALU.mult
                                            ).then_inc(ph.s("max"), 1)

                def weigh(u):
                    t, s = ph.units[u]
                    g = ph.nu * i + u
                    n = ph.nk(t)
                    ph.wait(ve, "exp", 2 * g + 2)
                    if u >= 4:
                        ph.wait(ve, "o_out", g - 3)
                    st.then(v.reciprocal(RCP[:, u % 4, 0:2], SUM[:, u % 4, 0:2]))
                    st.then(v.tensor_scalar(RCP[:, u % 4, 1:2], RCP[:, u % 4, 1:2], SUM[:, u % 4, 0:1], LAM[:, 3:4], ALU.mult, ALU.mult))
                    v.scalar_tensor_tensor(out=PR[:, u % 2, 0, 0:n], in0=PR[:, u % 2, 1, 0:n], scalar=RCP[:, u % 4, 1:2],
                                           in1=PR[:, u % 2, 0, 0:n], op0=ALU.mult, op1=ALU.add).then_inc(ph.s("probs"), 1)

                def take(u):
                    t, s = ph.units[u]
                    g = ph.nu * i + u
                    js, n0 = ph.jt(t)
                    n1 = len(js) - n0
                    ph.wait(ve, "probs_T", g + 1)
                    if u >= 2:
                        ph.wait(ve, "o", g - 1)
                    v.tensor_copy(PT[:, u % 2, n0:n0 + n1, :], PB[:, 5, 0:P * n1].rearrange("p (j n) -> p j n", j=n1)
                                  ).then_inc(ph.s("pt_d"), 1)

                def outs(u):
                    t, s = ph.units[u]
                    g = ph.nu * i + u
                    if ph.maps == 1:
                        if u >= 4:
                            ph.wait(ve, "o_out", g - 3)
                        if ph.local:
                            st.then(v.tensor_tensor(RCP[:, u % 4, 1:2], SUM[:, u % 4, 0:1], SUM[:, u % 4, 1:2], ALU.add))
                            st.then(v.reciprocal(RCP[:, u % 4, 0:1], RCP[:, u % 4, 1:2]))
                        else:
                            st.then(v.reciprocal(RCP[:, u % 4, 0:1], SUM[:, u % 4, 0:1]))
                    ph.wait(ve, "o", g + 1)
                    w = P if ph.maps == 2 else HD
                    v.tensor_scalar(OO[:, t, ds(col(i, s), w)], PB[:, 6 + u % 2, HD * s:HD * s + w], RCP[:, u % 4, 0:1], None, ALU.mult
                                    ).then_inc(ph.s("o_out"), 1)

                maxima(0)
                for u in range(ph.nu):
                    if ph.maps == 2:
                        weigh(u)
                    if u + 1 < ph.nu:
                        maxima(u + 1)
                    take(u)
                    if u:
                        outs(u - 1)
                outs(ph.nu - 1)

            def layer_norm(l, n, t, what, last=None):
                x = X[:, t, :]
                for h in range(2):
                    st.did(v.bn_stats(BN[:, h, :], x[:, 512 * h:512 * (h + 1)]))
                st.settle()
                st.then(v.bn_aggr(MV[:, 2:4], BN[:, :, :].rearrange("p a b -> p (a b)")))
                v.tensor_scalar(MV[:, 1:2], MV[:, 3:4], EPS, None, ALU.add).then_inc(S(f"{what}_ms"), 1)
                wait(ve, f"{what}_root", l, n + 1)
                st.then(v.tensor_scalar(x, x, MV[:, 2:3], MV[:, 1:2], ALU.subtract, ALU.mult))
                st.then(v.tensor_tensor(x, x, ROWS[:, ROW_LG, :], ALU.mult))
                ins = v.tensor_tensor(x, x, ROWS[:, ROW_LB, :], ALU.add)
                if last is None:
                    st.then(ins)
                else:
                    ins.then_inc(last, 1)

            def stage_c(l):
                tl = tiles_of[l]
                n_t = len(tl)
                cnt = [0]
                wait(ve, "rows", l, 8 * 16)

                def take(dst, n, router):
                    cnt[0] += 1
                    wait(ve, "cT", l, cnt[0])
                    if router and n >= 2:
                        wait(ve, "lg", l, n - 1)
                    v.tensor_copy(dst, PB[:, 5, :].rearrange("p (k n) -> p k n", k=4)).then_inc(S("cTd"), 1)

                def o_norm(n):
                    if l:
                        return
                    o = OO[:, tl[n], 0:512].rearrange("p (h n) -> p h n", h=4)
                    sq = SQ.rearrange("p (h n) -> p h n", h=4)
                    st.then(v.tensor_tensor(sq, o, o, ALU.mult))
                    st.then(v.tensor_reduce(MS[:, 4:8], sq, AX.X, ALU.add))
                    v.tensor_scalar(MS[:, 0:4], MS[:, 4:8], 1.0 / P, EPS, ALU.mult, ALU.add).then_inc(S("sub_ms"), 1)
                    ve.wait_ge(S("sub_root"), n + 1)
                    st.then(v.tensor_tensor(o, o, MS[:, 0:4].unsqueeze(2).to_broadcast([P, 4, P]), ALU.mult))
                    v.tensor_tensor(o, o, SUBG[:, :].unsqueeze(1).to_broadcast([P, 4, P]), ALU.mult).then_inc(S("o_normed"), 1)

                def o_t(n):
                    take(HT[:, 4:8, P * tl[n]:P * (tl[n] + 1)], n, False)

                o_norm(0)
                o_t(0)
                for n in range(n_t + 2):
                    if n + 1 < n_t:
                        o_norm(n + 1)
                        o_t(n + 1)
                    if 1 <= n <= n_t:
                        take(H2T[:, (n - 1) % 2, 4:8, :], n - 1, True)
                    if n < n_t:
                        t = tl[n]
                        m = m_of(t)
                        wait(ve, "mix", l, n + 1)
                        st.did(v.tensor_tensor(TMP[:, 0:512], PB[:, 2 * (n % 2), :], ROWS[:, ROW_G + m, 0:512], ALU.mult))
                        st.settle()
                        v.tensor_tensor(TMP[:, 512:1024], PB[:, 2 * (n % 2) + 1, :], ROWS[:, ROW_G + m, 512:1024], ALU.mult
                                        ).then_inc(S("mix_used"), 1)
                        wait(ve, "mix_used", l, n + 1)
                        st.then(v.scalar_tensor_tensor(out=X[:, t, :], in0=X[:, t, :], scalar=ALPHA, in1=TMP, op0=ALU.mult, op1=ALU.add))
                        layer_norm(l, n, t, "ln")
                        st.then(v.tensor_tensor(OO[:, t, :], X[:, t, :], ROWS[:, ROW_SC + m, :], ALU.mult))
                        v.tensor_tensor(OO[:, t, :], OO[:, t, :], ROWS[:, ROW_SH + m, :], ALU.add).then_inc(S("h2"), 1)

            def routing(l):
                T = len(MOE_TILES[l])
                wait(ve, "lg_out", l, T)
                wait(ve, "h2_stored", l, 16 * T)
                g = lambda n: grid(n)[:, 0:T, :]
                lg, le = LG[:, 0:T, 0:NG], LG[:, 0:T, NG:NG + NE]
                OH1, OH2, BOTH, MSK, T1, RANK = g(0), g(1), g(2), g(3), g(4), g(5)
                GE, GOH, J = grid(6, NG)[:, 0:T, :], grid(7, NG)[:, 0:T, :], g(8)
                small = OF[:, 2048 + 192 * 10:2048 + 192 * 10 + 8 * T].rearrange("p (a t) -> p a t", a=8)
                b3 = lambda a, w: a.unsqueeze(2).to_broadcast([P, T, w])
                row = lambda a, w=NE: a.unsqueeze(1).to_broadcast([P, T, w])

                def first_max(x, w, pr, oh, m):
                    st.then(v.tensor_reduce(m, x, AX.X, ALU.max))
                    st.then(v.tensor_tensor(oh, x, b3(m, w), ALU.is_equal))
                    st.then(v.tensor_tensor(oh, oh, row(pr, w), ALU.mult))
                    st.then(v.tensor_reduce(small[:, 7, :], oh, AX.X, ALU.max))
                    st.then(v.tensor_tensor(oh, oh, b3(small[:, 7, :], w), ALU.is_equal))

                first_max(lg, NG, prio4, GOH, small[:, 0, :])
                v.tensor_tensor(GE, lg, b3(small[:, 0, :], NG), ALU.subtract).then_inc(S("gmax"), 1)
                st.then(v.tensor_scalar(GOH, GOH, -1.0, -BIG_NEG, ALU.add, ALU.mult))
                st.then(v.tensor_tensor(MSK.rearrange("p t (g e) -> p t g e", g=NG), le.rearrange("p t (g e) -> p t g e", g=NG),
                                        GOH.unsqueeze(3).to_broadcast([P, T, NG, EPG]), ALU.add))
                first_max(MSK, NE, prio, OH1, small[:, 1, :])
                st.then(v.tensor_scalar(T1, OH1, BIG_NEG, None, ALU.mult))
                st.then(v.tensor_tensor(MSK, MSK, T1, ALU.add))
                first_max(MSK, NE, prio, OH2, small[:, 2, :])
                v.tensor_tensor(BOTH, OH1, OH2, ALU.add).then_inc(S("chosen"), 1)
                v.tensor_tensor(GATE[:, 1, 0:T], small[:, 2, :], small[:, 1, :], ALU.subtract).then_inc(S("top2"), 1)
                wait(ve, "gexp", l, 1)
                st.then(v.tensor_reduce(small[:, 3, :], GE, AX.X, ALU.add))
                wait(ve, "texp", l, 1)
                st.then(v.tensor_scalar(small[:, 4, :], GATE[:, 1, 0:T], 1.0, None, ALU.add))
                st.then(v.tensor_tensor(small[:, 4, :], small[:, 4, :], small[:, 3, :], ALU.mult))
                st.then(v.reciprocal(GATE[:, 0, 0:T], small[:, 4, :]))
                st.then(v.tensor_tensor(GATE[:, 1, 0:T], GATE[:, 1, 0:T], GATE[:, 0, 0:T], ALU.mult))
                wait(ve, "ranks", l, 1)
                ov = OF[:, 2048 + 192 * 10 + 48:2048 + 192 * 10 + 48 + 5 * NE].rearrange("p (a e) -> p a e", a=5)
                CNT, NOVE, END, BLK, ZERO = (ov[:, a, :] for a in range(5))
                st.did(v.tensor_copy(RANK.rearrange("p t e -> p (t e)"), PB[:, 6, 0:NE * T]))
                st.did(v.tensor_copy(CNT, PB[:, 6, 256:256 + NE]))
                st.did(v.memset(NOVE, 0.0))
                st.did(v.memset(J, 0.0))
                st.did(v.memset(ZERO, 1.0))
                st.settle()
                for j in range(1, JMAX + 1):
                    st.then(v.scalar_tensor_tensor(out=NOVE, in0=CNT, scalar=float(j * CAP), in1=NOVE, op0=ALU.is_gt, op1=ALU.add))
                    st.then(v.scalar_tensor_tensor(out=J, in0=RANK, scalar=float(j * CAP), in1=J, op0=ALU.is_ge, op1=ALU.add))
                st.then(v.tensor_tensor_scan(END, ZERO, NOVE, 0.0, ALU.mult, ALU.add))
                st.then(v.tensor_tensor(BLK, END, NOVE, ALU.subtract))
                st.then(v.tensor_tensor(BLK, BLK, iota, ALU.subtract))
                st.then(v.tensor_scalar(BLK, BLK, float(NE - 1), None, ALU.add))
                st.then(v.tensor_scalar(T1, J, 1.0, None, ALU.min))
                st.then(v.tensor_tensor(T1, T1, row(BLK), ALU.mult))
                st.then(v.tensor_tensor(T1, T1, J, ALU.add))
                st.then(v.tensor_tensor(T1, T1, row(iota), ALU.add))
                st.then(v.scalar_tensor_tensor(out=RANK, in0=J, scalar=-float(CAP), in1=RANK, op0=ALU.mult, op1=ALU.add))
                st.then(v.scalar_tensor_tensor(out=J, in0=RANK, scalar=float(NB), in1=T1, op0=ALU.mult, op1=ALU.add))
                for k, oh in enumerate((OH1, OH2)):
                    st.then(v.tensor_tensor(MSK, J, oh, ALU.mult))
                    st.then(v.tensor_reduce(small[:, 5, :], MSK, AX.X, ALU.add))
                    st.then(v.tensor_copy(ADI[:, k, 0:T], small[:, 5, :]))
                st.settle()
                big = OF[:, 2048:2048 + 16 * NE].rearrange("p (b e) -> p b e", b=16)
                st.then(v.tensor_tensor(big, END.unsqueeze(1).to_broadcast([P, 16, NE]),
                                        iota[:, 0:16].unsqueeze(2).to_broadcast([P, 16, NE]), ALU.is_le))
                st.then(v.tensor_reduce(ov[:, 0, 0:16], big, AX.X, ALU.add))
                st.then(v.tensor_scalar(ov[:, 0, 0:16], ov[:, 0, 0:16], float(NE - 1), None, ALU.min))
                st.did(v.tensor_copy(OVI[0:1, l, 0:16], ov[0:1, 0, 0:16]))
                st.settle()
                v.tensor_copy(OVI[0:1, l, 16:17], END[0:1, NE - 1:NE]).then_inc(S("routed"), 1)
                wait(ve, "slots", l, 16)
                v.tensor_scalar(IDT[0:CAP, :], IDX[0:CAP, :], 1, None, ALU.arith_shift_right).then_inc(S("tokens"), 1)

            def experts(l):
                def x_t(e, u, s_t, s_out, n):
                    wait(ve, s_t, l, n)
                    v.tensor_copy(XT[u][:, 4:8, 0:CAP], PB[:, 5, :].rearrange("p (k n) -> p k n", k=4)[:, :, 0:CAP]).then_inc(S(s_out), 1)

                def gate(u, n, s_sg, s_up, n_up, s_hx):
                    wait(ve, s_sg, l, n)
                    wait(ve, s_up, l, n_up)
                    v.tensor_tensor(HX[u], SG[u], PB[:, 2 * u + 1, 0:4 * CAP].rearrange("p (f n) -> p f n", f=4), ALU.mult).then_inc(S(s_hx), 1)

                def y_out(u, s_down, n, s_out):
                    wait(ve, s_down, l, n)
                    v.tensor_copy(YS[u][0:CAP, 512:1024], PB[0:CAP, 7, 0:512]).then_inc(S(s_out), 1)

                def main_x(e, u):
                    x_t(e, u, "xgT", "xTd", e + 1)

                def main_g(e, u):
                    gate(u, e + 1, "sg", "up_free", e + 3, "hx")

                def main_y(e, u, first=False):
                    if not first:
                        wait(ve, f"y_stored{u}", l, (e - u) * 8)
                    y_out(u, "down_free", e + 3, "y_d")
                main_x(0, 0)
                main_x(1, 1)
                main_g(0, 0)
                main_x(2, 0)
                main_g(1, 1)
                main_y(0, 0, True)
                main_x(3, 1)
                main_g(2, 0)
                main_y(1, 1, True)
                with ve.Fori(1, NE // 2 - 1) as i:
                    for u in (1, 0):
                        e = i * 2 + (1 if u else 2)
                        main_x(e + 1, 1 - u)
                        main_g(e, u)
                        main_y(e - 1, 1 - u)
                main_g(NE - 1, 1)
                main_y(NE - 2, 0)
                main_y(NE - 1, 1)
                def over_block(b, q):
                    x_t(q, 0, "over_xgT", "over_xTd", q + 1)
                    gate(0, q + 1, "over_sg", "over_up", q + 1, "over_hx")
                    y_out(0, "over_free", q + 2 + l, "over_yd")
                    lone_wait(ve, S("over_block"), q + 1)
                overflow(ve, l, over_block)

            def stage_f(l):
                wait(ve, "rowsf", l, 64)
                for n, t in enumerate(tiles_of[l]):
                    m = m_of(t)
                    wait(ve, f"yg{n % 2}", l, 16 * (n // 2 + 1))
                    y0, y1 = YG[n % 2][:, 0, :], YG[n % 2][:, 1, :]
                    st.then(v.tensor_scalar(y0, y0, GATE[:, 0, n:n + 1], None, ALU.mult))
                    st.then(v.scalar_tensor_tensor(out=y0, in0=y1, scalar=GATE[:, 1, n:n + 1], in1=y0, op0=ALU.mult, op1=ALU.add))
                    st.then(v.tensor_tensor(y0, y0, ROWS[:, ROW_G + m, :], ALU.mult))
                    v.scalar_tensor_tensor(out=X[:, t, :], in0=X[:, t, :], scalar=ALPHA, in1=y0, op0=ALU.mult, op1=ALU.add
                                           ).then_inc(S("yg_used"), 1)
                    wait(ve, "yg_used", l, n + 1)
                    layer_norm(l, n, t, "lnf", S("x_new"))

            stage_a(0)

            def loop(ph, per, body):
                with ve.Fori(0, ph.iters) as i:
                    st.enter(i, per)
                    body(i)
                st.leave(ph.iters)

            def a_body(i):
                for t in range(NT):
                    rope(PA, i, t, 0, 4, False)
                attention(PA, i, lambda i, s: i * P)

            def b_body(i):
                for t in range(NT):
                    rope(PBB, i, t, 1, 2, True)
                attention(PBB, i, lambda i, s: i * HD + 512 + 256 * s)

            loop(PA, NT * 3 + NT * 4, a_body)
            kv = Phase("kv", 1, [], 1, False)
            for t in range(NT):
                rope(kv, 0, t, 2, 2, True)
            ve.wait_ge(S("kv_rope"), NT)
            loop(PBB, NT * 6 + 12 * 2, b_body)
            stage_c(0)
            routing(0)
            experts(0)
            stage_f(0)
            stage_a(1)

            def n_body(i):
                ve.wait_ge(S("bias"), (i + 1) * 2)
                attention(PN, i, lambda i, s: i * P + HD * s)
            loop(PN, PN.nu * 4, n_body)
            stage_c(1)
            routing(1)
            experts(1)
            stage_f(1)


_INS = ["x", "c", "ctx", "c_ctx", "w_mod", "b_mod", "ln_g", "ln_b", "w_in_even", "w_out_even", "diff_lam", "diff_subln_g",
        "gqa_qk_g", "w_in_odd", "w_out_odd", "na_rpb", "router_g", "router_e", "w1", "w3", "w2"]


def shape_constants():
    import numpy as np

    c = np.zeros((P, C_W), np.float32)
    c[:, C_ID:C_ID + P] = np.eye(P)
    c[:, C_TRI:C_TRI + P] = np.triu(np.ones((P, P)), 1)
    c[:, C_ONE:C_ONE + P] = 1.0
    c[:, C_IOTA:C_IOTA + NE] = np.arange(NE)
    c[:, C_PRIO:C_PRIO + NE] = NE - np.arange(NE)
    c[:, C_PRIO4:C_PRIO4 + NG] = NG - np.arange(NG)
    c[:, C_TOK:C_TOK + NT] = 2 * (np.arange(P)[:, None] + P * np.arange(NT)[None, :])
    col = np.arange(P) % GRID_W
    first = np.clip(col - WIN_W // 2, 0, GRID_W - WIN_W)[:, None]
    key = np.arange(GRID_W)[None, :]
    c[:, C_MASK:C_MASK + GRID_W] = np.where((key >= first) & (key < first + WIN_W), 0.0, BIG_NEG)
    t = np.arange(SEQ)
    half = HD // 2
    inv = (np.float32(10000.0) ** (-np.arange(0, half, 2, dtype=np.float32) / np.float32(half))).astype(np.float32)
    ar = (t // GRID_W).astype(np.float32)[:, None] * inv
    ac = (t % GRID_W).astype(np.float32)[:, None] * inv
    ang = np.concatenate([ar, ar, ac, ac], -1)
    sign = np.repeat(np.array([-1, 1, -1, 1], np.float32), HD // 4)
    rope = np.zeros((P, NT, 2, HD), np.float32)
    rope[:, :NCT, 0, :] = 1.0
    rope[:, NCT:, 0, :] = np.cos(ang).reshape(SEQ // P, P, HD).transpose(1, 0, 2)
    rope[:, NCT:, 1, :] = (np.sin(ang) * sign).reshape(SEQ // P, P, HD).transpose(1, 0, 2)
    return {"consts": c, "rope": rope}


def kernel(**inputs):
    import numpy as np
    import concourse.bacc as bacc
    from concourse.bass_utils import run_bass_kernel_spmd

    nc = bacc.Bacc("TRN2", target_bir_lowering=False, num_devices=1)
    arrays = {n: np.ascontiguousarray(inputs[n]) for n in _INS}
    arrays.update(shape_constants())
    aps = {n: nc.dram_tensor(f"in_{n}", list(a.shape), mybir.dt.from_np(a.dtype), kind="ExternalInput").ap() for n, a in arrays.items()}
    out = nc.dram_tensor("out", [1, SEQ, D], mybir.dt.float32, kind="ExternalOutput").ap()
    build(nc, aps, out)
    r = run_bass_kernel_spmd(nc, [{f"in_{n}": a for n, a in arrays.items()}], core_ids=[0])
    return r.results[0]["out"]
```

```python
import math
from contextlib import ExitStack

import concourse.bass as bass
from concourse import mybir

P = 128
D = 1024
KT = D // P
SEQ, CTX = 512, 256
NTOK = CTX + SEQ
NT = NTOK // P
NCT = CTX // P
DEPTH = 2
MOE_TOK = [NTOK, SEQ]
GRID_W, ROWS_N, WIN_W = 64, SEQ // 64, 16
RPB_H, RPB_W = 15, 31
HD = 64
NE, NG, EPG = 32, 4, 8
ALPHA = (2.0 * DEPTH) ** 0.25
LAM_INIT = 0.8 - 0.6 * math.exp(0.0)
EPS = 1e-6
BIG_NEG = -1.0e30
CAP = 96
MUL = (1 << 16) // CAP + 1
assert all((r * MUL) >> 16 == r // CAP for r in range(NTOK))
NOV = (2 * NTOK - 1) // CAP
NB = NE + NOV
EMPTY = 1 << 20
C_ID, C_TRI, C_ONE, C_PRIO, C_PRIO4, C_MASK = 0, 128, 256, 384, 416, 420
C_SEL = C_MASK + 34
C_COUNT = C_SEL + 4
C_ENTRY = C_COUNT + CAP
C_W = C_ENTRY + 2 * NT
SLOT = 12288
Q0, K0, V0, BV0, P0, PT0, RS0, RT0, RO0 = 0, 1536, 2304, 3840, 4608, 7680, 9216, 9728, 10240
WC0 = SLOT
WO0 = SLOT
TA0 = SLOT + 8192
H2T0, TMP0 = TA0, TA0 + 2048


class Steps:

    def __init__(self, eng, sem):
        self.eng, self.sem, self.base, self.n = eng, sem, 0, 0

    def did(self, ins):
        ins.then_inc(self.sem, 1)
        self.n += 1

    def settle(self):
        self.eng.wait_ge(self.sem, self.base + self.n)

    def then(self, ins):
        self.did(ins)
        self.settle()

    def enter(self, i, per):
        self.outer, self.per = self.base + self.n, per
        self.base, self.n = self.outer + i * per, 0

    def leave(self, count):
        assert self.n == self.per, (self.n, self.per)
        self.base, self.n = self.outer + count * self.per, 0


def build(nc, A, out):
    f32, i32 = mybir.dt.float32, mybir.dt.int32
    ALU, ACT, AX = mybir.AluOpType, mybir.ActivationFunctionType, mybir.AxisListType
    ds = bass.ds
    ctx = ExitStack()

    def dram(name, shape, dt=f32):
        return nc.dram_tensor(name, shape, dt).ap()

    mod_d = [dram(f"mod_rows_{l}", [96, P]) for l in range(DEPTH)]
    h2_d = [dram(f"h2_rows_{l}", [MOE_TOK[l], D]) for l in range(DEPTH)]
    y_d = [dram(f"expert_rows_{l}", [2 * MOE_TOK[l], D]) for l in range(DEPTH)]
    RPB = RPB_H * RPB_W
    LR = 16 * RPB
    SKEW = LR + 7 * RPB_W + 15 + 32
    skew_d = dram("rpb_skewed", [P * SKEW + 64])

    with ctx:
        def sb(name, shape, dt=f32):
            return ctx.enter_context(nc.sbuf_tensor(name, shape, dt))

        sems = {}

        def S(name):
            if name not in sems:
                sems[name] = ctx.enter_context(nc.semaphore(name))
            return sems[name]

        X = sb("X", [P, NT, D])
        HT = sb("HT", [P, KT, NTOK])
        OO = sb("OO", [P, NT, D])
        ROWS = sb("ROWS", [P, 8, D])
        BIG = sb("BIG", [P, 2 * SLOT])
        CO = sb("CO", [P, C_W])
        SC = sb("SC", [P, KT, 2])
        MT = sb("MT", [P, DEPTH, 2, 48])
        LNT = sb("LNT", [P, 2, KT])
        LNT2 = sb("LNT2", [P, 2, KT])
        RW = sb("RW", [P, KT, NG + NE])
        LG = sb("LG", [P, NT, NG + NE])
        SUBG = sb("SUBG", [P, P])
        LAM = sb("LAM", [P, 4])
        NMX = sb("NMX", [P, 4, 4])
        SUM = sb("SUM", [P, 4, 4])
        RCP = sb("RCP", [P, 4, 4])
        MS = sb("MS", [P, 16])
        SUBMS = sb("SUBMS", [P, 2, 4])
        BN = sb("BN", [P, 2, 6])
        MV = sb("MV", [P, 4])
        MHALF = sb("MHALF", [P, 8])
        GATE = sb("GATE", [P, 2, NT])
        RJ = sb("RJ", [P, NT + 1, NE], i32)
        IX = sb("IX", [P, 2], i32)
        IY = sb("IY", [P, 2], i32)
        OVI = sb("OVI", [1, DEPTH, 20], i32)
        IDX = sb("IDX", [P, NB], i32)
        IDT = sb("IDT", [P, NB], i32)
        PB = ctx.enter_context(nc.psum_tensor("PB", [P, 8, 512], f32))
        PF = PB[:, :, :].rearrange("p b n -> p (b n)")
        HF = HT[:, :, :].rearrange("p k n -> p (k n)")
        OF = OO[:, :, :].rearrange("p k n -> p (k n)")

        ident = CO[:, C_ID:C_ID + P]
        tri = CO[:, C_TRI:C_TRI + P]
        ones = CO[:, C_ONE:C_ONE + P]
        count = CO[:, C_COUNT:C_COUNT + CAP]
        iota = count[:, 0:NE]
        entry = CO[:, C_ENTRY:C_ENTRY + 2 * NT].rearrange("p (k t) -> p k t", k=2)
        prio = CO[:, C_PRIO:C_PRIO + NE]
        prio4 = CO[:, C_PRIO4:C_PRIO4 + NG]
        colmask = CO[:, C_MASK:C_MASK + 32]
        tilemask = CO[:, C_MASK + 32:C_MASK + 34]

        WM = [BIG[:, 4096 * u:4096 * (u + 1)].rearrange("p (k n) -> p k n", k=KT) for u in range(4)]
        FOLD = BIG[:, 16384:17408].rearrange("p (m n) -> p m n", m=2)
        SEL = CO[:, C_SEL:C_SEL + 4].rearrange("p (m n) -> p m n", m=2)
        BM = [HF[0:2, :], ROWS[0:2, 0:6, :].rearrange("p a n -> p (a n)")]
        CROW = OF[0:4 * KT, 1056:1184]
        LMV = OF[:, 544:800].rearrange("p (a n) -> p a n", a=4)
        LMT = OF[:, 800:928].rearrange("p (a n) -> p a n", a=2)
        QG = OF[:, 928:1056].rearrange("p (a n) -> p a n", a=2)

        QT = BIG[:, Q0:Q0 + 1536].rearrange("p (s n) -> p s n", s=2)
        KTr, V = BIG[:, K0:K0 + 768], BIG[:, V0:V0 + 768].rearrange("p (t n) -> p t n", t=NT)
        BV = BIG[:, BV0:BV0 + 768].rearrange("p (t n) -> p t n", t=NT)
        BK = BIG[:, P0 + 1536:P0 + 3072].rearrange("p (s n) -> p s n", s=2)
        QQ = BIG[:, 0:3072].rearrange("p (i n) -> p i n", i=4)
        QC = BIG[:, RS0:RS0 + 768]
        WQ = BIG[:, WC0 + 3072:WC0 + 7168].rearrange("p (k n) -> p k n", k=KT)
        PR = BIG[:, P0:P0 + 3072].rearrange("p (u m n) -> p u m n", u=2, m=2)
        PT = BIG[:, PT0:PT0 + 1536].rearrange("p (u j n) -> p u j n", u=2, j=6)
        RS = BIG[:, RS0:RS0 + 512].rearrange("p (u n) -> p u n", u=2)
        RT = BIG[:, RT0:RT0 + 512].rearrange("p (u n) -> p u n", u=2)
        RO = BIG[:, RO0:RO0 + 512].rearrange("p (u n) -> p u n", u=2)
        RSW, RTW, ROW = (BIG[:, RS0 + 1024 * a:RS0 + 1024 * (a + 1)].rearrange("p (u n) -> p u n", u=2) for a in range(3))
        PR1 = BIG[:, P0:P0 + 1536].rearrange("p (u n) -> p u n", u=2)
        PR4 = BIG[:, P0:P0 + 2048].rearrange("p (u n) -> p u n", u=4)
        WC = [BIG[:, WC0 + 3072 * u:WC0 + 3072 * (u + 1)].rearrange("p (k n) -> p k n", k=KT) for u in range(2)]
        WO = [BIG[:, WO0 + 4096 * n:WO0 + 4096 * (n + 1)].rearrange("p (k n) -> p k n", k=KT) for n in range(2)]
        TAB = BIG[:, TA0:TA0 + 2304].rearrange("p (a t s n) -> p a t s n", a=3, t=NT, s=2)
        RAW = BIG[:, 9216:9216 + 2 * 256].rearrange("p (s n) -> p s n", s=2)
        GT = BIG[:, 9728:9728 + 2048].rearrange("p (s a n) -> p s a n", s=2, a=2)
        H2T = BIG[:, H2T0:H2T0 + 2048].rearrange("p (u k n) -> p u k n", u=2, k=KT)
        TMP = BIG[:, TMP0:TMP0 + 1024]
        SQ = BIG[:, TMP0 + 1024:TMP0 + 1536].rearrange("p (h n) -> p h n", h=4)

        W1 = [BIG[:, SLOT * u:SLOT * u + 4096].rearrange("p (k n) -> p k n", k=KT) for u in range(2)]
        W3 = [BIG[:, SLOT * u + 4096:SLOT * u + 8192].rearrange("p (k n) -> p k n", k=KT) for u in range(2)]
        W2 = [BIG[:, SLOT * u + 8192:SLOT * u + 12288].rearrange("p (k n) -> p k n", k=4) for u in range(2)]
        XG = [HF[:, 1024 * u:1024 * (u + 1)] for u in range(2)]
        XT = [HF[:, 2048 + 768 * u:2048 + 768 * (u + 1)].rearrange("p (k n) -> p k n", k=KT) for u in range(2)]
        SG = [HF[:, 3584 + 384 * u:3584 + 384 * (u + 1)].rearrange("p (k n) -> p k n", k=4) for u in range(2)]
        HX = [HF[:, 4352 + 384 * u:4352 + 384 * (u + 1)].rearrange("p (k n) -> p k n", k=4) for u in range(2)]
        YS = [OF[:, 1024 * u:1024 * (u + 1)] for u in range(2)]
        YG = [OF[:, 2048 * (u + 1):2048 * (u + 2)].rearrange("p (k n) -> p k n", k=2) for u in range(2)]

        SLOT_R = HF[:, 0:2 * NT * CAP].rearrange("p (k t r) -> p k t r", k=2, t=NT)
        SLOT_B = HF[:, 2 * NT * CAP:2 * NT * (CAP + NB)].rearrange("p (k t b) -> p k t b", k=2, t=NT)

        def grid(n, w=NE):
            return OF[:, 2048 + 192 * n:2048 + 192 * n + NT * w].rearrange("p (t e) -> p t e", t=NT)

        ROW_G, ROW_SC, ROW_SH, ROW_LG, ROW_LB = 0, 2, 4, 6, 7

        LAYER0 = dict(cT=12, cTa=12, cTd=12, chosen=1, down_free=NE + 2, down_loaded0=8 * NE, down_loaded1=8 * NE, gexp=1, gmax=1,
                      h2_stored=16 * NT, h2=NT, hTa=NT, slot_rows=2, table=1, y_scaled=NT, lnf_moved=NT, lnf_done=NT, hx=NE, ix=NE, iy=NE, tokens=1, lg_out=NT, lg=NT, mix_used=NT, mix=NT, ranks=1,
                      routed=1, rowsf=64, rows=128, rw_loaded=32, sg=NE, texp=1, top2=1,
                      up1=NE, up_free=NE + 2, up_loaded0=16 * NE, up_loaded1=16 * NE, wo_loaded=32, xTa=NE, xTd=NE,
                      xT=NT, x_new=NT, xgT=NE, xg0=8 * NE, xg1=8 * NE, y_all=1, y_a=NE, y_d=NE, y_stored0=8 * NE,
                      y_stored1=8 * NE, yg_used=NT, yg0=8 * NT, yg1=8 * NT, ln_ms=NT, ln_root=NT, lnf_ms=NT, lnf_root=NT)

        CREDIT = dict(y_a=1, y_d=1)

        def wait(eng, what, l, n):
            eng.wait_ge(S(what), n + l * LAYER0.get(what, 0) + CREDIT.get(what, 0))

        def lone_wait(eng, sem, n):
            eng.wait_ge(sem, n)
            eng.nop(nofuse=True)

        def overflow(eng, l, body):
            wait(eng, "routed", l, 1)
            n_over = eng.value_load(OVI[0:1, l, 16:17], min_val=0, max_val=NOV)
            prev = eng.value_load(OVI[0:1, 0, 16:17], min_val=0, max_val=NOV) if l else 0
            with eng.If(n_over > 0):
                with eng.Fori(0, NOV) as b:
                    with eng.If(b < n_over):
                        body(b, b + prev)

        def m_of(t):
            return 1 if t < NCT else 0

        def mod_row(l, part, m):
            return mod_d[l][48 * m + 8 * part:48 * m + 8 * part + 8, :].rearrange("j n -> (j n)").partition_broadcast(P)

        PIECES = [(NCT, slice(0, 64), 0), (NCT, slice(64, P), GRID_W - 8)] + [
            (NCT + j, slice(0, P), 16 * j - 8) for j in range(1, 4)]

        def cols(rows, col, part):
            n = (part.stop - part.start) // ROWS_N
            return rows.rearrange("(r c) d -> c r d", c=GRID_W)[col:col + n, :, :]

        def edge(a):
            return a.rearrange("p (a n) -> p a n", n=64)[:, 0:8:7, :]

        tiles_of = [list(range(NT)), list(range(NCT, NT))]
        MOE_TILES = tiles_of

        PER_MAP = ("scores", "max", "exp")
        UNIT_STEPS = PER_MAP + ("probs_T", "pt_a", "pt_d", "o", "o_out")

        class Phase:
            def __init__(self, name, iters, units, maps, local):
                self.name, self.iters, self.units, self.maps, self.local = name, iters, units, maps, local
                self.nu = len(units)
                self.ahead = 2 if local else 1
                self.rs, self.rt, self.ro = (RSW, RTW, ROW) if name in ("kv", "q0") else (RS, RT, RO)
                self.before = dict.fromkeys(UNIT_STEPS, 0)

            def s(self, what):
                return S(f"att_{what}" if what in UNIT_STEPS else f"{self.name}_{what}")

            def wait(self, eng, what, n):
                eng.wait_ge(self.s(what), n + (self.before[what] if what in UNIT_STEPS else 0))

            def after(self, other):
                for w in UNIT_STEPS:
                    self.before[w] = other.before[w] + other.iters * other.nu * (other.maps if w in PER_MAP else 1)
                return self

            def nk(self, t):
                return CTX if (t < NCT) else NTOK

            def jt(self, t):
                if self.local:
                    return ([2, 5, 0, 1] if t == NCT else [t - 1, t, 0, 1]), 4
                return ([0, 1], 1) if t < NCT else ([0, 1, 2, 3, 4, 5], 4)

            def region(self, u, m):
                if self.local:
                    return u % 4
                return 2 * m if self.maps == 2 else 2 * (u % 2)

        PA = Phase("a0", 4, [(t, 0) for t in [2, 0, 3, 4, 5, 1]], 2, False)
        PBB = Phase("b0", 4, [(t, s) for s in range(2) for t in [2, 3, 4, 5, 0, 1]], 1, False).after(PA)
        KV, QP = Phase("kv", 1, [], 1, False), Phase("q0", 1, [], 1, False)
        PN = Phase("n1", 8, [(t, s) for s in range(2) for t in range(NCT, NT)], 1, True).after(PBB)

        def rows_c(eng, l):
            for m in range(2):
                eng.dma_start(ROWS[:, ROW_G + m, :], mod_row(l, 2, m)).then_inc(S("rows"), 16)
                eng.dma_start(ROWS[:, ROW_SC + m, :], mod_row(l, 4, m)).then_inc(S("rows"), 16)
                eng.dma_start(ROWS[:, ROW_SH + m, :], mod_row(l, 3, m)).then_inc(S("rows"), 16)
            eng.dma_start(ROWS[:, ROW_LG, :], A["ln_g"][l, 0].partition_broadcast(P)).then_inc(S("rows"), 16)
            eng.dma_start(ROWS[:, ROW_LB, :], A["ln_b"][l, 0].partition_broadcast(P)).then_inc(S("rows"), 16)
            eng.dma_start(RW[:, :, 0:NG], A["router_g"][l].rearrange("(k p) n -> p k n", p=P)).then_inc(S("rw_loaded"), 16)
            eng.dma_start(RW[:, :, NG:NG + NE], A["router_e"][l].rearrange("(k p) n -> p k n", p=P)).then_inc(S("rw_loaded"), 16)

        block = ctx.enter_context(nc.Block())

        @block.sync
        def _(sp):
            for l in range(DEPTH):
                wm = A["w_mod"][l].rearrange("(k p) n -> p k n", p=P)
                def chunk(i, u):
                    sp.dma_start(WM[u], wm[:, :, ds(i * 2048 + 512 * u, 512)]).then_inc(S(f"wmod_loaded{u}"), 16)
                if l == 0:
                    sp.wait_ge(S("c_loaded"), 64)
                    sp.wait_ge(S("const_loaded"), 16)
                    for u in (1, 0, 2, 3):
                        chunk(0, u)
                with sp.Fori(0 if l else 1, 3) as i:
                    for u in (1, 0, 2, 3):
                        if u == 0:
                            lone_wait(sp, S("mod_folded"), 3 * l + i)
                        else:
                            sp.wait_ge(S("wmod_used"), 12 * l + i * 4 + (u - 4))
                        chunk(i, u)

            def head_weights(ph, src, parts, cols):
                with sp.Fori(0, ph.iters // 2) as i2:
                    for b in range(2):
                        i = i2 * 2 + b
                        ph.wait(sp, "w_free", i + 1)
                        for dst, width, start, step in parts:
                            sp.dma_start(WC[b][:, :, dst:dst + width], src[:, :, ds(start + i * step, width)]
                                         ).then_inc(ph.s(f"w_loaded{b}"), 16)

            def w_out(l, src):
                if l == 0:
                    sp.wait_ge(S("wo_free"), 1)
                else:
                    sp.wait_ge(S("n1_w_free"), 2 + PN.iters)
                for n in range(2):
                    sp.dma_start(WO[n], src[:, :, 512 * n:512 * (n + 1)]).then_inc(S("wo_loaded"), 16)

            def experts(l):
                w1 = A["w1"][l].rearrange("e (k p) f -> e p k f", p=P)
                w3 = A["w3"][l].rearrange("e (k p) f -> e p k f", p=P)
                w2 = A["w2"][l].rearrange("e (k p) f -> e p k f", p=P)

                def load_up(e, u):
                    wait(sp, "up_free", l, e + 1)
                    sp.dma_start(W1[u], w1[ds(e, 1)].rearrange("e p k f -> (e p) k f")).then_inc(S(f"up_loaded{u}"), 16)
                    sp.dma_start(W3[u], w3[ds(e, 1)].rearrange("e p k f -> (e p) k f")).then_inc(S(f"up_loaded{u}"), 16)

                def load_down(e, u):
                    wait(sp, "down_free", l, e + 1)
                    sp.dma_start(W2[u], w2[ds(e, 1)].rearrange("e p k f -> (e p) k f")).then_inc(S(f"down_loaded{u}"), 16)

                for e in range(2):
                    load_up(e, e)
                    load_down(e, e)
                load_up(2, 0)
                with sp.Fori(1, NE // 2 - 1) as i:
                    for u in (1, 0):
                        e = i * 2 + (1 if u else 2)
                        load_up(e, u)
                        load_down(e - 1, 1 - u)
                load_up(NE - 1, 1)
                load_down(NE - 2, 0)
                load_down(NE - 1, 1)
                def block_weights(b, q):
                    ex = sp.value_load(OVI[0:1, l, ds(b, 1)], min_val=0, max_val=NE - 1)
                    sp.wait_ge(S("over_free"), q + 1 + l)
                    sp.dma_start(W1[0], w1[ds(ex, 1)].rearrange("e p k f -> (e p) k f")).then_inc(S("over_loaded"), 16)
                    sp.dma_start(W3[0], w3[ds(ex, 1)].rearrange("e p k f -> (e p) k f")).then_inc(S("over_loaded"), 16)
                    sp.dma_start(W2[0], w2[ds(ex, 1)].rearrange("e p k f -> (e p) k f")).then_inc(S("over_loaded"), 16)
                overflow(sp, l, block_weights)

            we = A["w_in_even"][0].rearrange("(k p) n -> p k n", p=P)
            wd = A["w_in_odd"][0].rearrange("(k p) n -> p k n", p=P)
            head_weights(PA, we, [(0, 128, 0, 128), (128, 128, 512, 128), (256, 128, 1024, 128)], 384)
            sp.wait_ge(S("a0_w_free"), 5)
            sp.dma_start(WC[0][:, :, 0:256], we[:, :, 2048:2304]).then_inc(S("kv_loaded"), 16)
            sp.wait_ge(S("a0_w_free"), 6)
            for h in range(8):
                sp.dma_start(WQ[:, :, P * (h % 4) + HD * (h // 4):][:, :, 0:HD], we[:, :, 1536 + HD * h:1536 + HD * (h + 1)]
                             ).then_inc(S("wq_loaded"), 16)
            w_out(0, A["w_out_even"][0].rearrange("(k p) n -> p k n", p=P))
            experts(0)
            head_weights(PN, wd, [(0, 128, 0, 128), (128, 128, 1024, 128), (256, 128, 2048, 128)], 384)
            sp.wait_ge(S("x_new"), NT)
            rows_c(sp, 1)
            w_out(1, A["w_out_odd"][0].rearrange("(k p) n -> p k n", p=P))
            experts(1)

            for n, t in enumerate(tiles_of[1]):
                wait(sp, "x_new", 1, n + 1)
                for t_, half, col in PIECES:
                    if t_ == t:
                        sp.dma_start(cols(out[0], col, half), X[half, t, :]).then_inc(S("stored"), 16)
            sp.wait_ge(S("stored"), 16 * len(PIECES))

        @block.tensor
        def _(pe):
            mm = nc.tensor.matmul
            tr = nc.tensor.transpose
            pe.wait_ge(S("const_loaded"), 16)
            pe.wait_ge(S("c_loaded"), 64)
            tr(PB[:, 7, 0:4 * KT], CROW, ident[0:4 * KT, 0:4 * KT]).then_inc(S("c_T"), 1)
            pe.wait_ge(S("silu_c"), 1)
            for l in range(DEPTH):
                with pe.Fori(0, 3) as i:
                    for u in range(1, 4):
                        pe.wait_ge(S(f"wmod_loaded{u}"), (i + 1 + 3 * l) * 16)
                        pe.wait_ge(S("mod_added"), 12 * l + i * 4 + u)
                        for k in range(KT):
                            last = mm(PB[0:2, u - 1, :], SC[:, k, :], WM[u][:, k, :], start=k == 0, stop=k == KT - 1)
                        last.then_inc(S("wmod_used"), 1)
                    pe.wait_ge(S("mod_folded"), 3 * l + (i + 1))
                    pe.wait_ge(S("mod_added"), 12 * l + i * 4 + 4)
                    for m in range(2):
                        last = mm(PB[0:2, 3, :], SEL[:, m, :], FOLD[:, m, :], start=m == 0, stop=m == 1)
                    last.then_inc(S("wmod_used"), 1)

            def mod_columns(l):
                pe.wait_ge(S("mod_rows"), 2 * (l + 1))
                for j in range(48):
                    last = tr(PB[:, 4 + l, 2 * j:2 * j + 2], BM[l][:, P * j:P * (j + 1)], ident[0:2, 0:2])
                last.then_inc(S("mod_T"), 1)

            def stage_a(l):
                for n, t in enumerate(range(NT)):
                    if l == 0:
                        if t < NCT:
                            pe.wait_ge(S("ctx_loaded"), 16)
                        else:
                            pe.wait_ge(S("x_loaded"), 16 * len(PIECES))
                    else:
                        pe.wait_ge(S("lnf_done"), n + 1)
                    if n >= 2:
                        wait(pe, "hTa", l, n - 1)
                        if l == 0:
                            pe.wait_ge(S("hTd"), n - 1)
                    for k in range(KT):
                        last = tr(PB[:, 2 * (n % 2) + k // 4, P * (k % 4):P * (k % 4 + 1)], X[:, t, P * k:P * (k + 1)], ident)
                    last.then_inc(S("xT"), 1)
                wait(pe, "hTa", l, NT)
                if l == 0:
                    pe.wait_ge(S("hTd"), NT)

            def project_rows(ph, i, w, width, trs):
                def mms(t):
                    if t >= 2:
                        ph.wait(pe, "pj_out", 6 * i + t - 1)
                    for k in range(KT):
                        last = mm(PB[:, 6 + t % 2, 0:width], HT[:, k, P * t:P * (t + 1)], w[:, k, 0:width],
                                  start=k == 0, stop=k == KT - 1)
                    last.then_inc(ph.s("pj"), 1)

                def trans(t):
                    ph.wait(pe, "rope", 6 * i + t + 1)
                    if t >= 2:
                        ph.wait(pe, "qk_out", 6 * i + t - 1)
                    for n in range(trs):
                        last = tr(PB[:, 4 + t % 2, P * n:P * (n + 1)], ph.ro[:, t % 2, P * n:P * (n + 1)], ident)
                    last.then_inc(ph.s("qk_T"), 1)
                def late_v(b, tiles):
                    ph.wait(pe, "pj_out", 6 * i + 5 + b)
                    for c, t in enumerate(tiles):
                        for k in range(KT):
                            last = mm(PB[:, 6 + b, P * c:P * (c + 1)], HT[:, k, P * t:P * (t + 1)], w[:, k, width:width + P],
                                      start=k == 0, stop=k == KT - 1)
                    last.then_inc(ph.s("pv"), 1)

                for t in range(NT):
                    mms(t)
                    if t:
                        trans(t - 1)
                if ph is PA:
                    late_v(0, range(3))
                trans(NT - 1)
                return lambda: late_v(1, range(3, NT))

            def attention(ph, i, keys, v, q=None, meanwhile=None):
                def scores(u):
                    t, s = ph.units[u]
                    if ph.local and u >= 4:
                        ph.wait(pe, "max", ph.nu * i + u - 3)
                    if ph.maps == 1 and not ph.local and u >= 2:
                        ph.wait(pe, "exp", ph.nu * i + u - 1)
                    for m in range(ph.maps):
                        if ph.maps == 2 and u >= 1:
                            ph.wait(pe, "exp", (ph.nu * i + u - 1) * 2 + (m + 1))
                        r = ph.region(u, m)
                        qt = (q if q is not None else QT[:, m if ph.maps == 2 else s, :])[:, P * (t - (NCT if ph.local else 0)):][:, 0:P]
                        kt = keys if q is None else keys[:, s, :]
                        if ph.local:
                            a, b = (j - NCT for j in ph.jt(t)[0][0:2])
                            mm(PB[:, r, 0:P], qt, kt[:, CTX + P * a:CTX + P * (a + 1)], start=True, stop=True)
                            mm(PB[:, r, P:2 * P], qt, kt[:, CTX + P * b:CTX + P * (b + 1)], start=True, stop=True)
                            last = mm(PB[:, r, 256:512], qt, kt[:, 0:CTX], start=True, stop=True)
                        elif t < NCT:
                            last = mm(PB[:, r, 0:256], qt, kt[:, 0:CTX], start=True, stop=True)
                        else:
                            mm(PB[:, r, 0:512], qt, kt[:, 0:512], start=True, stop=True)
                            last = mm(PB[:, r + 1, 0:256], qt, kt[:, 512:NTOK], start=True, stop=True)
                        last.then_inc(ph.s("scores"), 1)

                def trans(u):
                    t, s = ph.units[u]
                    g = ph.nu * i + u
                    ph.wait(pe, "probs" if ph.maps == 2 else "exp", g + 1)
                    if ph.local and u >= 2:
                        ph.wait(pe, "pt_a", g - 1)
                    if not ph.local and u >= 1:
                        ph.wait(pe, "pt_a", g)
                        ph.wait(pe, "pt_d", g)
                    js, n0 = ph.jt(t)
                    src = PR[:, u % 2, 0, :] if ph.maps == 2 else PR4[:, u % 4, :] if ph.local else PR1[:, u % 2, :]
                    for j in range(len(js)):
                        b, c = (4 + (u % 2 if ph.local else 0), j) if j < n0 else (5, j - n0)
                        last = tr(PB[:, b, P * c:P * (c + 1)], src[:, P * j:P * (j + 1)], ident)
                    last.then_inc(ph.s("probs_T"), 1)

                def values(u):
                    t, s = ph.units[u]
                    g = ph.nu * i + u
                    ph.wait(pe, "pt_a", g + 1)
                    if not ph.local:
                        ph.wait(pe, "pt_d", g + 1)
                    if u >= 2:
                        ph.wait(pe, "o_out", g - 1)
                    js, n0 = ph.jt(t)
                    if ph is PA and u == 0:
                        ph.wait(pe, "v_out", 2 * (i + 1))
                    for j, kt_ in enumerate(js):
                        last = mm(PB[:, 6 + u % 2, 0:P], PT[:, u % 2, j, :], v[:, kt_, :],
                                  start=j == 0, stop=j == len(js) - 1)
                    last.then_inc(ph.s("o"), 1)

                for u in range(ph.ahead):
                    scores(u)
                if meanwhile is not None:
                    meanwhile()
                for u in range(ph.nu):
                    if u + ph.ahead < ph.nu:
                        scores(u + ph.ahead)
                    if u and ph is PA:
                        values(u - 1)
                    trans(u)
                    if u and ph is not PA:
                        values(u - 1)
                values(ph.nu - 1)
                ph.wait(pe, "o_out", ph.nu * (i + 1))

            def w_free(ph):
                for _ in range(2):
                    pe.nop(nofuse=True).then_inc(ph.s("w_free"), 1)

            def loop(ph, body):
                with pe.Fori(0, ph.iters // 2) as i2:
                    for b in range(2):
                        body(i2 * 2 + b, i2, b)

            def rows_iter(ph, width, trs, nw, kt, v):
                def body(i, i2, b):
                    ph.wait(pe, f"w_loaded{b}", (i2 + 1) * 16 * nw)
                    values_left = project_rows(ph, i, WC[b], width, trs)
                    ph.wait(pe, "qk_out", 6 * (i + 1))
                    attention(ph, i, kt, v, meanwhile=values_left)
                    pe.nop(nofuse=True).then_inc(ph.s("w_free"), 1)
                return body

            def odd_iter(i, i2, b):
                ph = PN
                ph.wait(pe, f"w_loaded{b}", (i2 + 1) * 48)
                w = WC[b]
                for k in range(KT):
                    last = mm(PB[:, 0, 0:512], w[:, k, 0:P], HT[:, k, CTX:NTOK], start=k == 0, stop=k == KT - 1)
                last.then_inc(ph.s("pq"), 1)
                for k in range(KT):
                    last = mm(PB[:, 1, 0:512], w[:, k, P:2 * P], HT[:, k, 0:512], start=k == 0, stop=k == KT - 1)
                last.then_inc(ph.s("pq"), 1)
                for k in range(KT):
                    last = mm(PB[:, 2, 0:256], w[:, k, P:2 * P], HT[:, k, 512:NTOK], start=k == 0, stop=k == KT - 1)
                last.then_inc(ph.s("pq"), 1)
                for t in range(NT):
                    bank, c = (6, t) if t < 4 else (7, t - 4)
                    for k in range(KT):
                        last = mm(PB[:, bank, P * c:P * (c + 1)], HT[:, k, P * t:P * (t + 1)], w[:, k, 2 * P:3 * P],
                                  start=k == 0, stop=k == KT - 1)
                    if t in (3, 5):
                        last.then_inc(ph.s("pq"), 1)
                ph.wait(pe, "qkv_out", 5 * (i + 1))
                pe.nop(nofuse=True).then_inc(ph.s("w_free"), 1)
                attention(ph, i, KTr, V)

            def stage_c(l):
                tl = tiles_of[l]
                n_t = len(tl)
                nth = [0]

                def bank45(src, ready):
                    ready()
                    if nth[0]:
                        wait(pe, "cTa", l, nth[0])
                        wait(pe, "cTd", l, nth[0])
                    for k in range(KT):
                        last = tr(PB[:, 4 + k // 4, P * (k % 4):P * (k % 4 + 1)], src[:, P * k:P * (k + 1)], ident)
                    last.then_inc(S("cT"), 1)
                    nth[0] += 1
                    return nth[0]

                def o_t(n):
                    return bank45(OO[:, tl[n], :], (lambda: pe.wait_ge(S("o_normed"), n + 1)) if l == 0 else (lambda: None))

                def h_t(n):
                    return bank45(OO[:, tl[n], :], lambda: wait(pe, "h2", l, n + 1))

                def mix(n, done):
                    wait(pe, "cTa", l, done)
                    wait(pe, "cTd", l, done)
                    if n >= 2:
                        wait(pe, "mix_used", l, n - 1)
                    t = tl[n]
                    for h in range(2):
                        for k in range(KT):
                            last = mm(PB[:, 2 * (n % 2) + h, 0:512], HT[:, k, P * t:P * (t + 1)], WO[h][:, k, :],
                                      start=k == 0, stop=k == KT - 1)
                    last.then_inc(S("mix"), 1)

                def route(n, done):
                    wait(pe, "cTa", l, done)
                    wait(pe, "cTd", l, done)
                    if n >= 2:
                        wait(pe, "lg_out", l, n - 1)
                    for k in range(KT):
                        last = mm(PB[:, 6 + n % 2, 0:NG + NE], H2T[:, n % 2, k, :], RW[:, k, :], start=k == 0, stop=k == KT - 1)
                    last.then_inc(S("lg"), 1)

                o_done = {0: o_t(0)}
                wait(pe, "wo_loaded", l, 32)
                wait(pe, "rw_loaded", l, 32)
                h_done = {}
                for n in range(n_t + 2):
                    if n < n_t:
                        if n + 1 < n_t:
                            o_done[n + 1] = o_t(n + 1)
                        mix(n, o_done[n])
                    if n >= 2:
                        route(n - 2, h_done[n - 2])
                    if 1 <= n <= n_t:
                        h_done[n - 1] = h_t(n - 1)
                    if n == n_t:
                        pe.nop(nofuse=True).then_inc(S("up_free"), 1)
                wait(pe, "lg_out", l, n_t)
                pe.nop(nofuse=True).then_inc(S("down_free"), 1)

            def ranks(l):
                tl = MOE_TILES[l]
                wait(pe, "chosen", l, 1)
                n = NE * len(tl)
                both = grid(2)[:, 0:len(tl), :].rearrange("p t e -> p (t e)")
                mm(PB[:, 6, 0:n], tri, both, start=True, stop=True)
                last = mm(PB[:, 6, 256:256 + n], ones, both, start=True, stop=True)
                last.then_inc(S("ranks"), 1)
                for k in range(2):
                    wait(pe, "slot_rows", l, k + 1)
                    for n in range(len(tl)):
                        last = mm(PB[0:CAP, 7, 0:NB], SLOT_R[:, k, n, :], SLOT_B[:, k, n, :],
                                  start=k == 0 and n == 0, stop=k == 1 and n == len(tl) - 1)
                last.then_inc(S("table"), 1)

            def experts(l):
                def x_t(e, u):
                    wait(pe, f"xg{u}", l, (e + 2 - u) * 8)
                    for k in range(KT):
                        last = tr(PB[:, 4 + k // 4, P * (k % 4):P * (k % 4) + CAP], XG[u][0:CAP, P * k:P * (k + 1)],
                                  ident[0:CAP, 0:CAP])
                    last.then_inc(S("xgT"), 1)

                def up(e, u, xt_a, xt_d, loaded, free):
                    loaded()
                    wait(pe, xt_a, l, e + 1)
                    wait(pe, xt_d, l, e + 1)
                    for w, (W, bank) in enumerate(((W1[u], 0), (W3[u], 1))):
                        for f in range(4):
                            for k in range(KT):
                                last = mm(PB[:, 2 * u + bank, CAP * f:CAP * (f + 1)], W[:, k, P * f:P * (f + 1)],
                                          XT[u][:, k, 0:CAP], start=k == 0, stop=k == KT - 1)
                        last.then_inc(S(free[w]), 1)

                def down(e, u, hx, loaded, out_a, out_d, done):
                    wait(pe, hx, l, e + 1)
                    loaded()
                    if out_a is not None:
                        wait(pe, out_a, l, e)
                        wait(pe, out_d, l, e)
                    for h in range(2):
                        for f in range(4):
                            last = mm(PB[0:CAP, 6 + h, 0:512], HX[u][:, f, 0:CAP], W2[u][:, f, 512 * h:512 * (h + 1)],
                                      start=f == 0, stop=f == 3)
                    last.then_inc(S(done), 1)

                def main_up(e, u):
                    up(e, u, "xTa", "xTd", lambda: wait(pe, f"up_loaded{u}", l, (e + 2 - u) * 16),
                       ("up1", "up_free"))

                def main_down(e, u):
                    down(e, u, "hx", lambda: wait(pe, f"down_loaded{u}", l, (e + 2 - u) * 8),
                         "y_a", "y_d", "down_free")

                x_t(0, 0)
                wait(pe, "xTa", l, 1)
                wait(pe, "xTd", l, 1)
                x_t(1, 1)
                main_up(0, 0)
                with pe.Fori(0, NE // 2 - 1) as i:
                    for u in (1, 0):
                        e = i * 2 + (1 if u else 2)
                        wait(pe, "xTa", l, e + 1)
                        wait(pe, "xTd", l, e + 1)
                        x_t(e + 1, 1 - u)
                        main_up(e, u)
                        main_down(e - 1, 1 - u)
                main_up(NE - 1, 1)
                main_down(NE - 2, 0)
                main_down(NE - 1, 1)

                wait(pe, "y_a", l, NE)
                wait(pe, "y_d", l, NE)
                pe.nop(nofuse=True).then_inc(S("over_free"), 1)

                def over_block(b, q):
                    pe.wait_ge(S("over_xg"), (q + 1) * 16)
                    for k in range(KT):
                        last = tr(PB[:, 4 + k // 4, P * (k % 4):P * (k % 4) + CAP], XG[0][0:CAP, P * k:P * (k + 1)],
                                  ident[0:CAP, 0:CAP])
                    last.then_inc(S("over_xgT"), 1)
                    up(q, 0, "over_xTa", "over_xTd", lambda: pe.wait_ge(S("over_loaded"), (q + 1) * 48), ("over_up1", "over_up"))
                    down(q, 0, "over_hx", lambda: None, None, None, "over_free")
                overflow(pe, l, over_block)

            mod_columns(0)
            pe.wait_ge(S("mod_rows"), 3)
            w_free(PA)
            stage_a(0)
            mod_columns(1)
            loop(PA, rows_iter(PA, 256, 2, 3, KTr, V))
            pe.wait_ge(S("kv_loaded"), 16)
            project_rows(KV, 0, WC[0], 256, 1)
            pe.wait_ge(S("kv_qk_out"), 6)
            pe.wait_ge(S("wq_loaded"), 16 * 8)
            project_rows(QP, 0, WQ, 512, 4)

            pe.wait_ge(S("q0_qk_out"), NT)
            pe.nop(nofuse=True).then_inc(S("wo_free"), 1)
            with pe.Fori(0, PBB.iters) as i:
                pe.wait_ge(S("q_copied"), i + 1)
                attention(PBB, i, BK, BV, QC)
            for name in ("up_free", "down_free"):
                pe.nop(nofuse=True).then_inc(S(name), 1)
            stage_c(0)
            ranks(0)
            experts(0)
            wait(pe, "y_all", 0, 1)
            w_free(PN)
            stage_a(1)
            loop(PN, odd_iter)
            for name in ("up_free", "down_free"):
                pe.nop(nofuse=True).then_inc(S(name), 1)
            stage_c(1)
            ranks(1)
            experts(1)

        @block.scalar
        def _(act):
            fn = nc.scalar.activation
            act.nop(nofuse=True).then_inc(S("y_a"), CREDIT["y_a"])
            act.dma_start(CO[:, :], A["consts"]).then_inc(S("const_loaded"), 16)
            act.dma_start(CROW[0:KT, :], A["c"].rearrange("o (k p) -> (o k) p", p=P)).then_inc(S("c_loaded"), 16)
            act.dma_start(CROW[KT:2 * KT, :], A["c_ctx"].rearrange("(k p) -> k p", p=P)).then_inc(S("c_loaded"), 16)
            act.dma_start(CROW[2 * KT:3 * KT, :], A["ln_g"][0, 1].rearrange("(k p) -> k p", p=P)).then_inc(S("c_loaded"), 16)
            act.dma_start(CROW[3 * KT:4 * KT, :], A["ln_b"][0, 1].rearrange("(k p) -> k p", p=P)).then_inc(S("c_loaded"), 16)
            for l in range(DEPTH):
                act.dma_start(BM[l], A["b_mod"][l].partition_broadcast(2)).then_inc(S("bmod_loaded"), 16)
            act.dma_start(QG[:, :, :].rearrange("p a n -> p (a n)"), A["gqa_qk_g"][0].rearrange("a n -> (a n)").partition_broadcast(P)).then_inc(S("small_loaded"), 16)
            act.dma_start(SUBG[:, :], A["diff_subln_g"][0].partition_broadcast(P)).then_inc(S("small_loaded"), 16)
            act.dma_start(LMV[:, :, :].rearrange("p a n -> p (a n)"), A["diff_lam"][0].rearrange("a n -> (a n)").partition_broadcast(P)).then_inc(S("small_loaded"), 16)

            act.wait_ge(S("c_T"), 1)
            fn(SC[:, :, :], PB[:, 7, 0:2 * KT].rearrange("p (m k) -> p k m", m=2), ACT.Silu).then_inc(S("silu_c"), 1)
            fn(LNT[:, :, :], PB[:, 7, 2 * KT:4 * KT].rearrange("p (a k) -> p a k", a=2), ACT.Copy).then_inc(S("lnt"), 1)
            act.wait_ge(S("lam_dots"), 1)
            fn(LAM[:, 0:2], LAM[:, 0:2], ACT.Exp).then_inc(S("lam_exp"), 1)
            act.wait_ge(S("wmod_used"), 8)
            act.dma_start(X[:, 0:NCT, :], A["ctx"][0].rearrange("(t p) d -> p t d", p=P)).then_inc(S("ctx_loaded"), 16)
            for t, half, col in PIECES:
                act.dma_start(X[half, t, :], cols(A["x"][0], col, half)).then_inc(S("x_loaded"), 16)
            act.dma_start(TAB[:, 0, :, :, :], A["rope"]).then_inc(S("rope_loaded"), 16)
            for l in range(DEPTH):
                act.wait_ge(S("mod_rows"), 2 * (l + 1))
                act.dma_start(mod_d[l].rearrange("(m j) p -> m (j p)", m=2), BM[l]).then_inc(S(f"mod_stored{l}"), 16)
            act.wait_ge(S("mod_ready"), 1)
            act.wait_ge(S("mod_stored0"), 16)

            def rows_f(l):
                for m in range(2):
                    act.dma_start(ROWS[:, ROW_G + m, :], mod_row(l, 5, m)).then_inc(S("rowsf"), 16)
                act.dma_start(ROWS[:, ROW_LG, :], A["ln_g"][l, 1].partition_broadcast(P)).then_inc(S("rowsf"), 16)
                act.dma_start(ROWS[:, ROW_LB, :], A["ln_b"][l, 1].partition_broadcast(P)).then_inc(S("rowsf"), 16)

            def modulate(l, n):
                m = m_of(n)
                wait(act, "xT", l, n + 1)
                for k in range(KT if l else 4):
                    src = PB[:, 2 * (n % 2) + k // 4, P * (k % 4):P * (k % 4 + 1)]
                    dst = HT[:, k, P * n:P * (n + 1)]
                    if l and n == NCT:
                        src, dst = src.rearrange("p (a n) -> p a n", a=2), edge(HT[:, k, CTX:NTOK])
                    elif l and n > NCT:
                        dst = HT[:, k, P * n - HD:P * (n + 1) - HD]
                    last = fn(dst, src, ACT.Identity,
                              bias=MT[:, l, m, k:k + 1], scale=MT[:, l, m, 8 + k:9 + k])
                last.then_inc(S("hTa"), 1)

            def stage_f(l):
                n_t = len(tiles_of[l])

                yt = y_d[l].rearrange("(t p k) d -> t p k d", p=P, k=2)

                def load(n):
                    if n < n_t:
                        act.dma_start(YG[n % 2], yt[n]).then_inc(S(f"yg{n % 2}"), 16)

                def scale(n):
                    wait(act, f"yg{n % 2}", l, 16 * (n // 2 + 1))
                    y0 = YG[n % 2][:, 0, :]
                    fn(y0, y0, ACT.Copy, scale=GATE[:, 0, n:n + 1]).then_inc(S("y_scaled"), 1)

                wait(act, "y_all", l, 1)
                load(0)
                load(1)
                scale(0)
                for n, t in enumerate(tiles_of[l]):
                    if n + 1 < n_t:
                        scale(n + 1)
                    wait(act, "lnf_moved", l, n + 1)
                    fn(X[:, t, :], X[:, t, :], ACT.Identity, bias=MV[:, 0:1], scale=MV[:, 1:2]).then_inc(S("lnf_done"), 1)
                    wait(act, "yg_used", l, n + 1)
                    load(n + 2)
                    if l + 1 < DEPTH and n:
                        modulate(l + 1, n - 1)
                if l + 1 < DEPTH:
                    modulate(l + 1, n_t - 1)

            def project_rows(ph, i, wqk, vdst, kdst, qdst, between=None):
                def take(t):
                    ph.wait(act, "pj", 6 * i + t + 1)
                    if t >= 2:
                        ph.wait(act, "rope", 6 * i + t - 1)
                    if vdst is not None:
                        fn(vdst[:, t, :], PB[:, 6 + t % 2, wqk:wqk + P], ACT.Copy)
                    fn(ph.rs[:, t % 2, 0:wqk], PB[:, 6 + t % 2, 0:wqk], ACT.Copy).then_inc(ph.s("pj_out"), 1)

                def give(t):
                    ph.wait(act, "qk_T", 6 * i + t + 1)
                    n = 0
                    if ph is QP:
                        last = fn(QQ[:, :, P * t:P * (t + 1)], PB[:, 4 + t % 2, :].rearrange("p (i n) -> p i n", i=4), ACT.Copy,
                                  scale=HD ** -0.5)
                    elif ph is KV:
                        for s in range(2):
                            h = slice(HD * s, HD * (s + 1))
                            last = fn(BK[h, s, P * t:P * (t + 1)], PB[h, 4 + t % 2, 0:P], ACT.Copy)
                    elif qdst is not None:
                        for s in range(2):
                            h = slice(HD * s, HD * (s + 1))
                            last = fn(qdst[h, s, P * t:P * (t + 1)], PB[h, 4 + t % 2, 0:P], ACT.Copy, scale=HD ** -0.5)
                        n = 1
                    if kdst is not None:
                        last = fn(kdst[:, P * t:P * (t + 1)], PB[:, 4 + t % 2, P * n:P * (n + 1)], ACT.Copy)
                    last.then_inc(ph.s("qk_out"), 1)
                def late_v(b, tiles):
                    ph.wait(act, "pv", 2 * i + (b + 1))
                    fn(V[:, tiles, :], PB[:, 6 + b, 0:P * (tiles.stop - tiles.start)].rearrange("p (t n) -> p t n", n=P), ACT.Copy
                       ).then_inc(ph.s("v_out"), 1)

                for t in range(NT):
                    take(t)
                    if between is not None:
                        between(t)
                    if t:
                        give(t - 1)
                if ph is PA:
                    late_v(0, slice(0, 3))
                give(NT - 1)
                return lambda: late_v(1, slice(3, NT))

            def attention(ph, i, meanwhile=None):
                def exps(u):
                    t, s = ph.units[u]
                    g = ph.nu * i + u
                    if u >= 2 and not ph.local:
                        ph.wait(act, "probs_T", g - 1)
                    if u >= 4:
                        ph.wait(act, "o_out", g - 3)
                    for m in range(ph.maps):
                        r = ph.region(u, m)
                        ph.wait(act, "max", ph.maps * g + m + 1)
                        nm = NMX[:, u % 4, m:m + 1]
                        if ph.local:
                            fn(PR4[:, u % 4, :], PR4[:, u % 4, :], ACT.Exp, bias=nm,
                               accum_out=SUM[:, u % 4, 0:1]).then_inc(ph.s("exp"), 1)
                        else:
                            n = ph.nk(t)
                            dst = PR[:, u % 2, m, 0:n] if ph.maps == 2 else PR1[:, u % 2, 0:n]
                            fn(dst, PF[:, 512 * r:512 * r + n], ACT.Exp, bias=nm,
                               accum_out=SUM[:, u % 4, m:m + 1]).then_inc(ph.s("exp"), 1)

                def take(u):
                    t, s = ph.units[u]
                    g = ph.nu * i + u
                    js, n0 = ph.jt(t)
                    ph.wait(act, "probs_T", g + 1)
                    if u >= 2:
                        ph.wait(act, "o", g - 1)
                    fn(PT[:, u % 2, 0:n0, :], PB[:, 4 + (u % 2 if ph.local else 0), 0:P * n0].rearrange("p (j n) -> p j n", j=n0), ACT.Copy
                       ).then_inc(ph.s("pt_a"), 1)
                exps(0)
                if meanwhile is not None:
                    meanwhile()
                for u in range(ph.nu):
                    if ph is PBB:
                        take(u)
                    if u + 1 < ph.nu:
                        exps(u + 1)
                    if ph is not PBB:
                        take(u)

            def stage_c(l):
                tl = tiles_of[l]
                n_t = len(tl)
                cnt = [0]

                def o_t(n):
                    cnt[0] += 1
                    wait(act, "cT", l, cnt[0])
                    t = tl[n]
                    fn(HT[:, 0:4, P * t:P * (t + 1)], PB[:, 4, :].rearrange("p (k n) -> p k n", k=4), ACT.Copy).then_inc(S("cTa"), 1)

                def h_t(n):
                    cnt[0] += 1
                    wait(act, "cT", l, cnt[0])
                    if n >= 2:
                        wait(act, "lg", l, n - 1)
                    fn(H2T[:, n % 2, 0:4, :], PB[:, 4, :].rearrange("p (k n) -> p k n", k=4), ACT.Copy).then_inc(S("cTa"), 1)

                o_t(0)
                for n in range(n_t + 2):
                    if n + 1 < n_t:
                        o_t(n + 1)
                    if 1 <= n <= n_t:
                        wait(act, "h2", l, n)
                        act.dma_start(h2_d[l][P * (n - 1):P * n, :], OO[:, tl[n - 1], :]).then_inc(S("h2_stored"), 16)
                        h_t(n - 1)
                    if n >= 2:
                        wait(act, "lg", l, n - 1)
                        fn(LG[:, n - 2, :], PB[:, 6 + n % 2, 0:NG + NE], ACT.Copy).then_inc(S("lg_out"), 1)

            def routing(l):
                wait(act, "gmax", l, 1)
                n = len(MOE_TILES[l])
                fn(grid(6, NG)[:, 0:n, :], grid(6, NG)[:, 0:n, :], ACT.Exp).then_inc(S("gexp"), 1)
                wait(act, "top2", l, 1)
                fn(GATE[:, 1, 0:n], GATE[:, 1, 0:n], ACT.Exp).then_inc(S("texp"), 1)

            def experts(l):
                def x_t(e, u, s_t, s_out):
                    wait(act, s_t, l, e + 1)
                    fn(XT[u][:, 0:4, 0:CAP], PB[:, 4, :].rearrange("p (k n) -> p k n", k=4)[:, :, 0:CAP], ACT.Copy).then_inc(S(s_out), 1)

                def gate(e, u, s_up, s_sg):
                    wait(act, s_up, l, e + 1)
                    fn(SG[u], PB[:, 2 * u, 0:4 * CAP].rearrange("p (f n) -> p f n", f=4), ACT.Silu).then_inc(S(s_sg), 1)

                def y_out(e, u, s_down, base, s_out):
                    wait(act, s_down, l, base + e + 1)
                    fn(YS[u][0:CAP, 0:512], PB[0:CAP, 6, 0:512], ACT.Copy).then_inc(S(s_out), 1)

                def main_y(e, u, first=False):
                    if not first:
                        wait(act, f"y_stored{u}", l, (e - u) * 8)
                    y_out(e, u, "down_free", 2, "y_a")

                s_t, s_o, s_u, s_g = "xgT", "xTa", "up1", "sg"
                x_t(0, 0, s_t, s_o)
                x_t(1, 1, s_t, s_o)
                gate(0, 0, s_u, s_g)
                x_t(2, 0, s_t, s_o)
                gate(1, 1, s_u, s_g)
                main_y(0, 0, True)
                x_t(3, 1, s_t, s_o)
                gate(2, 0, s_u, s_g)
                main_y(1, 1, True)
                with act.Fori(1, NE // 2 - 1) as i:
                    for u in (1, 0):
                        e = i * 2 + (1 if u else 2)
                        x_t(e + 1, 1 - u, s_t, s_o)
                        gate(e, u, s_u, s_g)
                        main_y(e - 1, 1 - u)
                gate(NE - 1, 1, s_u, s_g)
                main_y(NE - 2, 0)
                main_y(NE - 1, 1)
                for u in range(2):
                    wait(act, f"y_stored{u}", l, NE * 8)

                def over_block(b, q):
                    x_t(q, 0, "over_xgT", "over_xTa")
                    gate(q, 0, "over_up1", "over_sg")
                    y_out(q, 0, "over_free", 1 + l, "over_ya")
                    lone_wait(act, S("over_block"), q + 1)
                overflow(act, l, over_block)

            for n in range(NT):
                modulate(0, n)
            act.wait_ge(S("mod_ready"), 2)
            act.wait_ge(S("mod_stored1"), 16)
            rows_c(act, 0)

            def half(ph, body):
                with act.Fori(0, ph.iters) as i:
                    body(i)

            half(PA, lambda i: attention(PA, i, project_rows(PA, i, 256, None, KTr, QT)))
            project_rows(KV, 0, 128, BV, None, None)
            def squares(t):
                if t == 0:
                    PA.wait(act, "o_out", PA.nu * PA.iters)
                else:
                    act.wait_ge(S("o_normed"), t)
                for h in range(4):
                    last = fn(SQ[:, h, :], OO[:, t, P * h:P * (h + 1)], ACT.Square, accum_out=SUBMS[:, 0, h:h + 1])
                last.then_inc(S("squared"), 1)

            project_rows(QP, 0, 512, None, None, None, squares)
            act.wait_ge(S("q0_qk_out"), NT)

            def pair(i):
                fn(QC.unsqueeze(1), QQ[:, ds(i, 1), :], ACT.Copy).then_inc(S("q_copied"), 1)
                attention(PBB, i)
            half(PBB, pair)
            stage_c(0)
            act.wait_ge(S("h2"), NT)
            rows_f(0)
            routing(0)
            experts(0)
            stage_f(0)

            def odd(i):
                ph = PN
                ph.wait(act, "pq", 5 * i + 1)
                for s in range(2):
                    h = slice(HD * s, HD * (s + 1))
                    fn(QT[h, s, 0:P].rearrange("p (a n) -> p a n", a=2), edge(PB[h, 0, :]), ACT.Copy, scale=HD ** -0.5)
                    last = fn(QT[h, s, P:512], PB[h, 0, 64:448], ACT.Copy, scale=HD ** -0.5)
                last.then_inc(ph.s("qkv_out"), 1)
                ph.wait(act, "pq", 5 * i + 2)
                fn(KTr[:, 0:512], PB[:, 1, :], ACT.Copy).then_inc(ph.s("qkv_out"), 1)
                ph.wait(act, "pq", 5 * i + 3)
                fn(KTr[:, 512:768], PB[:, 2, 0:256], ACT.Copy).then_inc(ph.s("qkv_out"), 1)
                ph.wait(act, "pq", 5 * i + 4)
                fn(V[:, 0:4, :], PB[:, 6, :].rearrange("p (t n) -> p t n", t=4), ACT.Copy).then_inc(ph.s("qkv_out"), 1)
                ph.wait(act, "pq", 5 * i + 5)
                fn(V[:, 4:6, :], PB[:, 7, 0:256].rearrange("p (t n) -> p t n", t=2), ACT.Copy).then_inc(ph.s("qkv_out"), 1)
                attention(ph, i)
            half(PN, odd)
            stage_c(1)
            wait(act, "h2", 1, 4)
            rows_f(1)
            routing(1)
            experts(1)
            stage_f(1)

        @block.gpsimd
        def _(po):
            tt = nc.gpsimd.tensor_tensor
            nc.gpsimd.memset(MHALF[:, :], -0.5).then_inc(S("mhalf"), 1)
            po.wait_ge(S("a0_pj"), NT)
            rpb = A["na_rpb"]
            for start, first, n in ((0, 0, LR), (-8, 0, 8), (LR, 0, 16)):
                dst = bass.AP(skew_d.tensor, 8 + start, [[8 * SKEW + 1, 16], [SKEW + RPB_W, 8], [1, n]])
                src = bass.AP(rpb.tensor, first, [[0, 16], [0, 8], [1, n]])
                po.dma_start(dst, src).then_inc(S("skewed"), 16)
            po.wait_ge(S("mhalf"), 1)

            def root(what, n, lo, hi, src):
                po.wait_ge(S(f"{what}_ms"), n)
                tt(src[:, lo:hi], src[:, lo:hi], MHALF[:, 0:hi - lo], ALU.pow).then_inc(S(f"{what}_root"), 1)

            def roots(what, count):
                with po.Fori(0, count) as n:
                    root(what, n + 1, 0, 2, MS)
            def norm_heads(t):
                o = OO[:, t, 0:512].rearrange("p (h n) -> p h n", h=4)
                po.wait_ge(S("squared"), t + 1)
                nc.gpsimd.tensor_scalar(SUBMS[:, 1, :], SUBMS[:, 0, :], 1.0 / P, EPS, ALU.mult, ALU.add).then_inc(S("sub_steps"), 1)
                po.wait_ge(S("sub_steps"), 3 * t + 1)
                tt(SUBMS[:, 1, :], SUBMS[:, 1, :], MHALF[:, 0:4], ALU.pow).then_inc(S("sub_steps"), 1)
                po.wait_ge(S("sub_steps"), 3 * t + 2)
                tt(o, o, SUBMS[:, 1, :].unsqueeze(2).to_broadcast([P, 4, P]), ALU.mult).then_inc(S("sub_steps"), 1)
                po.wait_ge(S("sub_steps"), 3 * t + 3)
                tt(o, o, SUBG[:, :].unsqueeze(1).to_broadcast([P, 4, P]), ALU.mult).then_inc(S("o_normed"), 1)

            roots("kv", NT)
            for t in range(NT):
                if t:
                    norm_heads(t - 1)
                root("q0", t + 1, 0, 8, MS)
            norm_heads(NT - 1)
            def layer(l):
                tl = tiles_of[l]
                for n in range(len(tl)):
                    root("ln", n + 1 + l * NT, 1, 2, MV)
                wait(po, "h2_stored", l, 16 * len(tl))
                wait(po, "tokens", l, 1)

                def gather(col, u, s_ix, n_ix, s_x):
                    nc.gpsimd.tensor_copy(IX[0:CAP, u:u + 1], IDT[0:CAP, ds(col, 1)]).then_inc(S(s_ix), 1)
                    lone_wait(po, S(s_ix), n_ix + l * LAYER0.get(s_ix, 0))
                    po.indirect_dma_start(XG[u][0:CAP, :], None, h2_d[l], bass.IndirectOffsetOnAxis(ap=IX[0:CAP, u:u + 1], axis=0),
                                          bounds_check=MOE_TOK[l] - 1, oob_is_err=False).then_inc(S(s_x), 16)

                def scatter(col, u, s_iy, n_iy, s_y):
                    nc.gpsimd.tensor_copy(IY[0:CAP, u:u + 1], IDX[0:CAP, ds(col, 1)]).then_inc(S(s_iy), 1)
                    lone_wait(po, S(s_iy), n_iy + l * LAYER0.get(s_iy, 0))
                    po.indirect_dma_start(y_d[l], bass.IndirectOffsetOnAxis(ap=IY[0:CAP, u:u + 1], axis=0), YS[u][0:CAP, :], None,
                                          bounds_check=2 * MOE_TOK[l] - 1, oob_is_err=False).then_inc(S(s_y), 16)

                def main_scatter(e, u):
                    wait(po, "y_a", l, e + 1)
                    wait(po, "y_d", l, e + 1)
                    scatter(e, u, "iy", e + 1, f"y_stored{u}")
                for e in range(4):
                    if e >= 2:
                        wait(po, "xgT", l, e - 1)
                    gather(e, e % 2, "ix", e + 1, f"xg{e % 2}")
                with po.Fori(2, NE // 2) as i:
                    for u in range(2):
                        e = i * 2 + u
                        wait(po, "xgT", l, e - 1)
                        gather(e, u, "ix", e + 1, f"xg{u}")
                        main_scatter(e - 4, u)
                for e in range(NE - 4, NE):
                    main_scatter(e, e % 2)
                wait(po, "xgT", l, NE)
                for u in range(2):
                    wait(po, f"y_stored{u}", l, NE * 8)

                def over_block(b, q):
                    po.wait_ge(S("over_free"), q + 1 + l)
                    gather(b + NE, 0, "over_ix", q + 1, "over_xg")
                    po.wait_ge(S("over_ya"), q + 1)
                    po.wait_ge(S("over_yd"), q + 1)
                    scatter(b + NE, 0, "over_iy", q + 1, "over_stored")
                    po.wait_ge(S("over_stored"), (q + 1) * 16)
                    po.nop(nofuse=True).then_inc(S("over_block"), 1)
                overflow(po, l, over_block)
                po.nop(nofuse=True).then_inc(S("y_all"), 1)
                for n in range(len(tl)):
                    root("lnf", n + 1 + l * NT, 1, 2, MV)

            layer(0)

            po.wait_ge(S("skewed"), 48)
            nc.gpsimd.memset(GT[:, :, :, 256:512], 0.0).then_inc(S("gt_zero"), 1)
            po.wait_ge(S("gt_zero"), 1)
            with po.Fori(0, PN.iters) as i:
                po.wait_ge(S("n1_w_free"), i + 2)
                po.wait_ge(PN.s("max"), i * PN.nu + PN.before["max"])
                src = bass.AP(skew_d.tensor, 8 + 7 * RPB_W + 7, [[SKEW, P], [RPB, 16], [1, 249]])
                po.dma_start(RAW[:, :, 0:249], src[:, ds(i * 2, 2), :]).then_inc(S("raw"), 16)
                po.wait_ge(S("raw"), (i + 1) * 16)
                for s in range(2):
                    def run(first, n):
                        r = RAW[:, s, first:first + 1]
                        return bass.AP(r.tensor, r.offset, [list(r.ap[0]), [1, n], [RPB_W, 8]])
                    g = lambda a, lo, n: GT[:, s, a, lo:lo + 8 * n].rearrange("p (m r) -> p m r", r=8)
                    tt(g(0, 0, 32), run(0, 32), colmask.unsqueeze(2).to_broadcast([P, 32, 8]), ALU.add).then_inc(S("bias"), 1)
                    for a in range(2):
                        tt(g(1, P * a, 16), run(8, 16), tilemask[:, a:a + 1].unsqueeze(2).to_broadcast([P, 16, 8]), ALU.add
                           ).then_inc(S("bias"), 1)
            layer(1)

        @block.vector
        def _(ve):
            v = nc.vector
            st = Steps(ve, S("dve_steps"))
            ve.nop(nofuse=True).then_inc(S("y_d"), CREDIT["y_d"])
            ve.nop(nofuse=True).then_inc(S("mod_added"), 4)
            ve.wait_ge(S("small_loaded"), 48)
            ve.wait_ge(S("const_loaded"), 16)
            st.then(v.tensor_tensor(LMT[:, :, :], LMV[:, 0:4:2, :], LMV[:, 1:4:2, :], ALU.mult))
            v.tensor_reduce(LAM[:, 0:2], LMT[:, :, :], AX.X, ALU.add).then_inc(S("lam_dots"), 1)
            ve.wait_ge(S("lam_exp"), 1)
            st.then(v.tensor_tensor(LAM[:, 2:3], LAM[:, 1:2], LAM[:, 0:1], ALU.subtract))
            st.then(v.tensor_scalar(LAM[:, 3:4], LAM[:, 2:3], -LAM_INIT, None, ALU.add))
            st.did(v.tensor_scalar(SUBG[:, :], SUBG[:, :], 1.0 - LAM_INIT, None, ALU.mult))
            st.settle()
            def clear_q():
                st.did(v.memset(QT[HD:P, 0, :], 0.0))
                st.then(v.memset(QT[0:HD, 1, :], 0.0))

            ve.wait_ge(S("bmod_loaded"), 32)
            ve.wait_ge(S("silu_c"), 1)
            for l in range(DEPTH):
                with ve.Fori(0, 3) as i:
                    st.enter(i, 2 * KT - 2)
                    ve.wait_ge(S("wmod_loaded0"), (i + 1 + 3 * l) * 16)
                    for k in range(KT):
                        for m in range(2):
                            w, f, c = WM[0][:, k, :], FOLD[:, m, :], SC[:, k, m:m + 1]
                            if k == 0:
                                st.did(v.tensor_scalar(f, w, c, None, ALU.mult))
                            else:
                                ins = v.scalar_tensor_tensor(out=f, in0=w, scalar=c, in1=f, op0=ALU.mult, op1=ALU.add)
                                if k < KT - 1:
                                    st.did(ins)
                        if k < KT - 1:
                            st.settle()
                        elif m == 1:
                            ins.then_inc(S("mod_folded"), 1)
                    for n, u in enumerate((1, 2, 3, 0)):
                        part = BM[l][:, ds(i * 2048 + 512 * u, 512)]
                        ve.wait_ge(S("wmod_used"), 12 * l + i * 4 + (n + 1))
                        v.tensor_tensor(part, part, PB[0:2, u - 1 if u else 3, :], ALU.add).then_inc(S("mod_added"), 1)
                st.leave(3)
                ve.wait_ge(S("mod_added"), 4 + 12 * (l + 1))
                for a in (1, 4):
                    part = BM[l][:, D * a:D * (a + 1)]
                    v.tensor_scalar(part, part, 1.0, None, ALU.add).then_inc(S("mod_rows"), 1)
            clear_q()
            for l in range(DEPTH):
                ve.wait_ge(S("mod_T"), l + 1)
                v.tensor_copy(MT[:, l, :, :], PB[:, 4 + l, 0:96].rearrange("p (j m) -> p m j", m=2)).then_inc(S("mod_ready"), 1)
                if l == 0:
                    ve.wait_ge(S("mod_ready"), 1)
                    ve.wait_ge(S("mod_stored0"), 16)
                    for n in range(NT):
                        m = m_of(n)
                        ve.wait_ge(S("xT"), n + 1)
                        for k in range(4, KT):
                            last = v.tensor_scalar(HT[:, k, P * n:P * (n + 1)], PB[:, 2 * (n % 2) + 1, P * (k - 4):P * (k - 3)],
                                                   MT[:, 0, m, 8 + k:9 + k], MT[:, 0, m, k:k + 1], ALU.mult, ALU.add)
                        last.then_inc(S("hTd"), 1)
            ve.wait_ge(S("mod_ready"), 2)
            ve.wait_ge(S("lnt"), 1)
            for m in range(2):
                shift, scale = MT[:, 1, m, 0:KT], MT[:, 1, m, KT:2 * KT]
                st.then(v.tensor_tensor(LNT2[:, m, :], LNT[:, 1, :], scale, ALU.mult))
                st.then(v.tensor_tensor(shift, shift, LNT2[:, m, :], ALU.add))
                st.then(v.tensor_tensor(scale, scale, LNT[:, 0, :], ALU.mult))
            ve.wait_ge(S("rope_loaded"), 16)
            for a in range(2):
                g = QG[:, a, :]
                st.did(v.tensor_tensor(TAB[:, 1 + a, :, 0, :], TAB[:, 0, :, 0, :], g.unsqueeze(1).to_broadcast([P, NT, HD]), ALU.mult))
                for half in range(2):
                    gs = g.rearrange("p (b h n) -> p b h n", b=2, h=2)[:, :, 1 - half, :]
                    dst = TAB[:, 1 + a, :, 1, :].rearrange("p t (b h n) -> p t b h n", b=2, h=2)[:, :, :, half, :]
                    src = TAB[:, 0, :, 1, :].rearrange("p t (b h n) -> p t b h n", b=2, h=2)[:, :, :, half, :]
                    st.did(v.tensor_tensor(dst, src, gs.unsqueeze(1).to_broadcast([P, NT, 2, 16]), ALU.mult))
            st.settle()
            def rope(ph, i, t, tab, groups, norm):
                w = HD * groups
                if t:
                    ph.wait(ve, "rope", 6 * i + t)
                ph.wait(ve, "pj_out", 6 * i + t + 1)
                x = ph.rs[:, t % 2, 0:w].rearrange("p (g n) -> p g n", g=groups)
                r1 = ph.rt[:, 0, 0:w].rearrange("p (g n) -> p g n", g=groups)
                r2 = ph.rt[:, 1, 0:w].rearrange("p (g n) -> p g n", g=groups)
                if norm:
                    st.then(v.tensor_tensor(r1, x, x, ALU.mult))
                    st.then(v.tensor_reduce(MS[:, 8:8 + groups], r1, AX.X, ALU.add))
                    v.tensor_scalar(MS[:, 0:groups], MS[:, 8:8 + groups], 1.0 / HD, EPS, ALU.mult, ALU.add).then_inc(ph.s("ms"), 1)
                st.did(v.tensor_tensor(r1, x, TAB[:, tab, t, 0, :].unsqueeze(1).to_broadcast([P, groups, HD]), ALU.mult))
                for half in range(2):
                    xs = x.rearrange("p g (b h n) -> p g b h n", b=2, h=2)[:, :, :, 1 - half, :]
                    sn = TAB[:, tab, t, 1, :].rearrange("p (b h n) -> p b h n", b=2, h=2)[:, :, half, :]
                    dst = r2.rearrange("p g (b h n) -> p g b h n", b=2, h=2)[:, :, :, half, :]
                    st.did(v.tensor_tensor(dst, xs, sn.unsqueeze(1).to_broadcast([P, groups, 2, 16]), ALU.mult))
                st.settle()
                if t >= 2:
                    ph.wait(ve, "qk_T", 6 * i + t - 1)
                dst = ph.ro[:, t % 2, 0:w].rearrange("p (g n) -> p g n", g=groups)
                if norm:
                    st.then(v.tensor_tensor(r1, r1, r2, ALU.add))
                    ph.wait(ve, "root", 6 * i + t + 1)
                    v.tensor_tensor(dst, r1, MS[:, 0:groups].unsqueeze(2).to_broadcast([P, groups, HD]), ALU.mult).then_inc(ph.s("rope"), 1)
                else:
                    v.tensor_tensor(dst, r1, r2, ALU.add).then_inc(ph.s("rope"), 1)

            def attention(ph, i, col):
                def maxima(u):
                    t, s = ph.units[u]
                    g = ph.nu * i + u
                    if u >= 4:
                        ph.wait(ve, "max", ph.maps * (g - 3))
                    for m in range(ph.maps):
                        r = ph.region(u, m)
                        ph.wait(ve, "scores", ph.maps * g + m + 1)
                        if ph.local:
                            if u >= 4:
                                ph.wait(ve, "probs_T", g - 3)
                            ve.nop(nofuse=True)
                            st.then(v.tensor_tensor_reduce(out=PR4[:, u % 4, :], in0=PB[:, r, :], in1=GT[:, s, 1 if t == NCT else 0, :],
                                                           scale=1.0, scalar=BIG_NEG, op0=ALU.add, op1=ALU.max,
                                                           accum_out=RCP[:, u % 4, 3:4]))
                            v.tensor_scalar(NMX[:, u % 4, 0:1], RCP[:, u % 4, 3:4], -1.0, None, ALU.mult).then_inc(ph.s("max"), 1)
                        else:
                            v.tensor_reduce(NMX[:, u % 4, m:m + 1], PF[:, 512 * r:512 * r + ph.nk(t)], AX.X, ALU.max, negate=True
                                            ).then_inc(ph.s("max"), 1)

                def weigh(u):
                    t, s = ph.units[u]
                    g = ph.nu * i + u
                    n = ph.nk(t)
                    ph.wait(ve, "exp", 2 * g + 2)
                    if u >= 4:
                        ph.wait(ve, "o_out", g - 3)
                    st.then(v.reciprocal(RCP[:, u % 4, 0:2], SUM[:, u % 4, 0:2]))
                    st.then(v.tensor_scalar(RCP[:, u % 4, 1:2], RCP[:, u % 4, 1:2], SUM[:, u % 4, 0:1], LAM[:, 3:4], ALU.mult, ALU.mult))
                    v.scalar_tensor_tensor(out=PR[:, u % 2, 0, 0:n], in0=PR[:, u % 2, 1, 0:n], scalar=RCP[:, u % 4, 1:2],
                                           in1=PR[:, u % 2, 0, 0:n], op0=ALU.mult, op1=ALU.add).then_inc(ph.s("probs"), 1)

                def take(u):
                    t, s = ph.units[u]
                    g = ph.nu * i + u
                    js, n0 = ph.jt(t)
                    n1 = len(js) - n0
                    ph.wait(ve, "probs_T", g + 1)
                    if u >= 2:
                        ph.wait(ve, "o", g - 1)
                    v.tensor_copy(PT[:, u % 2, n0:n0 + n1, :], PB[:, 5, 0:P * n1].rearrange("p (j n) -> p j n", j=n1)
                                  ).then_inc(ph.s("pt_d"), 1)

                def outs(u):
                    t, s = ph.units[u]
                    g = ph.nu * i + u
                    if ph.maps == 1:
                        if u >= 4:
                            ph.wait(ve, "o_out", g - 3)
                        ph.wait(ve, "exp", g + 1)
                        st.then(v.reciprocal(RCP[:, u % 4, 0:1], SUM[:, u % 4, 0:1]))
                    ph.wait(ve, "o", g + 1)
                    w = P if ph.maps == 2 else HD
                    v.tensor_scalar(OO[:, t, ds(col(i, s), w)], PB[:, 6 + u % 2, HD * s:HD * s + w], RCP[:, u % 4, 0:1], None, ALU.mult
                                    ).then_inc(ph.s("o_out"), 1)

                for u in range(ph.ahead):
                    maxima(u)
                for u in range(ph.nu):
                    if ph.maps == 2:
                        weigh(u)
                    if u + ph.ahead < ph.nu:
                        maxima(u + ph.ahead)
                    if not ph.local:
                        take(u)
                    if u:
                        outs(u - 1)
                outs(ph.nu - 1)

            def layer_norm(l, n, t, what):
                x = X[:, t, :]
                for h in range(2):
                    st.did(v.bn_stats(BN[:, h, :], x[:, 512 * h:512 * (h + 1)]))
                st.settle()
                st.then(v.bn_aggr(MV[:, 2:4], BN[:, :, :].rearrange("p a b -> p (a b)")))
                v.tensor_scalar(MV[:, 1:2], MV[:, 3:4], EPS, None, ALU.add).then_inc(S(f"{what}_ms"), 1)
                wait(ve, f"{what}_root", l, n + 1)
                st.then(v.tensor_scalar(x, x, MV[:, 2:3], MV[:, 1:2], ALU.subtract, ALU.mult))
                st.then(v.tensor_tensor(x, x, ROWS[:, ROW_LG, :], ALU.mult))
                st.then(v.tensor_tensor(x, x, ROWS[:, ROW_LB, :], ALU.add))

            def stage_c(l):
                tl = tiles_of[l]
                n_t = len(tl)
                cnt = [0]
                wait(ve, "rows", l, 8 * 16)

                def take(dst, n, router):
                    cnt[0] += 1
                    wait(ve, "cT", l, cnt[0])
                    if router and n >= 2:
                        wait(ve, "lg", l, n - 1)
                    v.tensor_copy(dst, PB[:, 5, :].rearrange("p (k n) -> p k n", k=4)).then_inc(S("cTd"), 1)

                def o_t(n):
                    take(HT[:, 4:8, P * tl[n]:P * (tl[n] + 1)], n, False)

                o_t(0)
                for n in range(n_t + 2):
                    if n + 1 < n_t:
                        o_t(n + 1)
                    if 1 <= n <= n_t:
                        take(H2T[:, (n - 1) % 2, 4:8, :], n - 1, True)
                    if n < n_t:
                        t = tl[n]
                        m = m_of(t)
                        wait(ve, "mix", l, n + 1)
                        st.did(v.tensor_tensor(TMP[:, 0:512], PB[:, 2 * (n % 2), :], ROWS[:, ROW_G + m, 0:512], ALU.mult))
                        st.settle()
                        v.tensor_tensor(TMP[:, 512:1024], PB[:, 2 * (n % 2) + 1, :], ROWS[:, ROW_G + m, 512:1024], ALU.mult
                                        ).then_inc(S("mix_used"), 1)
                        wait(ve, "mix_used", l, n + 1)
                        st.then(v.scalar_tensor_tensor(out=X[:, t, :], in0=X[:, t, :], scalar=ALPHA, in1=TMP, op0=ALU.mult, op1=ALU.add))
                        layer_norm(l, n, t, "ln")
                        st.then(v.tensor_tensor(OO[:, t, :], X[:, t, :], ROWS[:, ROW_SC + m, :], ALU.mult))
                        v.tensor_tensor(OO[:, t, :], OO[:, t, :], ROWS[:, ROW_SH + m, :], ALU.add).then_inc(S("h2"), 1)

            def routing(l):
                T = len(MOE_TILES[l])
                wait(ve, "lg_out", l, T)
                wait(ve, "h2_stored", l, 16 * T)
                g = lambda n: grid(n)[:, 0:T, :]
                lg, le = LG[:, 0:T, 0:NG], LG[:, 0:T, NG:NG + NE]
                OH1, OH2, BOTH, MSK, T1 = g(0), g(1), g(2), g(3), g(4)
                GE, GOH = grid(6, NG)[:, 0:T, :], grid(7, NG)[:, 0:T, :]
                small = OF[:, 2048 + 192 * 10:2048 + 192 * 10 + 8 * T].rearrange("p (a t) -> p a t", a=8)
                b3 = lambda a, w: a.unsqueeze(2).to_broadcast([P, T, w])
                row = lambda a, w=NE: a.unsqueeze(1).to_broadcast([P, T, w])

                def first_max(x, w, pr, oh, m):
                    st.then(v.tensor_reduce(m, x, AX.X, ALU.max))
                    st.then(v.tensor_tensor(oh, x, b3(m, w), ALU.is_equal))
                    st.then(v.tensor_tensor(oh, oh, row(pr, w), ALU.mult))
                    st.then(v.tensor_reduce(small[:, 7, :], oh, AX.X, ALU.max))
                    st.then(v.tensor_tensor(oh, oh, b3(small[:, 7, :], w), ALU.is_equal))

                first_max(lg, NG, prio4, GOH, small[:, 0, :])
                v.tensor_tensor(GE, lg, b3(small[:, 0, :], NG), ALU.subtract).then_inc(S("gmax"), 1)
                st.then(v.tensor_scalar(GOH, GOH, -1.0, -BIG_NEG, ALU.add, ALU.mult))
                st.then(v.tensor_tensor(MSK.rearrange("p t (g e) -> p t g e", g=NG), le.rearrange("p t (g e) -> p t g e", g=NG),
                                        GOH.unsqueeze(3).to_broadcast([P, T, NG, EPG]), ALU.add))
                first_max(MSK, NE, prio, OH1, small[:, 1, :])
                st.then(v.tensor_scalar(T1, OH1, BIG_NEG, None, ALU.mult))
                st.then(v.tensor_tensor(MSK, MSK, T1, ALU.add))
                first_max(MSK, NE, prio, OH2, small[:, 2, :])
                v.tensor_tensor(BOTH, OH1, OH2, ALU.add).then_inc(S("chosen"), 1)
                v.tensor_tensor(GATE[:, 1, 0:T], small[:, 2, :], small[:, 1, :], ALU.subtract).then_inc(S("top2"), 1)
                wait(ve, "gexp", l, 1)
                st.then(v.tensor_reduce(small[:, 3, :], GE, AX.X, ALU.add))
                wait(ve, "texp", l, 1)
                st.then(v.tensor_scalar(small[:, 4, :], GATE[:, 1, 0:T], 1.0, None, ALU.add))
                st.then(v.tensor_tensor(small[:, 4, :], small[:, 4, :], small[:, 3, :], ALU.mult))
                st.then(v.reciprocal(GATE[:, 0, 0:T], small[:, 4, :]))
                st.then(v.tensor_tensor(GATE[:, 1, 0:T], GATE[:, 1, 0:T], GATE[:, 0, 0:T], ALU.mult))
                wait(ve, "ranks", l, 1)
                ov = OF[:, 2048 + 192 * 10 + 48:2048 + 192 * 10 + 48 + 5 * NE].rearrange("p (a e) -> p a e", a=5)
                END, BLK, ZERO = (ov[:, a, :] for a in range(2, 5))
                RC = OF[:, 4352:4352 + 224].rearrange("p (t e) -> p t e", e=NE)[:, 0:T + 1, :]
                RCJ = OF[:, 4608:4608 + 224].rearrange("p (t e) -> p t e", e=NE)[:, 0:T + 1, :]
                BEFORE = OF[:, 4864:4864 + 224].rearrange("p (t e) -> p t e", e=NE)[:, 0:T + 1, :]
                st.did(v.memset(ZERO, 1.0))
                st.then(v.memset(BEFORE[:, 0, :], 0.0))
                for n in range(1, T + 1):
                    st.then(v.tensor_tensor(BEFORE[:, n, :], BEFORE[:, n - 1, :], PB[:, 6, 256 + NE * (n - 1):256 + NE * n], ALU.add))
                st.did(v.tensor_tensor(RC[:, 0:T, :].rearrange("p t e -> p (t e)"), BEFORE[:, 0:T, :].rearrange("p t e -> p (t e)"),
                                       PB[:, 6, 0:NE * T], ALU.add))
                st.then(v.tensor_scalar(RC[:, T, :], BEFORE[:, T, :], -1.0, 0.0, ALU.add, ALU.max))
                st.then(v.tensor_scalar(RCJ, RC, float(MUL), None, ALU.mult))
                st.then(v.tensor_copy(RJ[:, 0:T + 1, :], RCJ))
                st.then(v.tensor_scalar(RJ[:, 0:T + 1, :], RJ[:, 0:T + 1, :], 16, None, ALU.arith_shift_right))
                st.then(v.tensor_copy(RCJ, RJ[:, 0:T + 1, :]))
                RANK, J, NOVE = RC[:, 0:T, :], RCJ[:, 0:T, :], RCJ[:, T, :]
                st.then(v.tensor_tensor_scan(END, ZERO, NOVE, 0.0, ALU.mult, ALU.add))
                st.then(v.tensor_tensor(BLK, END, NOVE, ALU.subtract))
                st.then(v.tensor_tensor(BLK, BLK, iota, ALU.subtract))
                st.then(v.tensor_scalar(BLK, BLK, float(NE - 1), None, ALU.add))
                st.then(v.tensor_scalar(T1, J, 1.0, None, ALU.min))
                st.then(v.tensor_tensor(T1, T1, row(BLK), ALU.mult))
                st.then(v.tensor_tensor(T1, T1, J, ALU.add))
                st.then(v.tensor_tensor(T1, T1, row(iota), ALU.add))
                st.then(v.scalar_tensor_tensor(out=RANK, in0=J, scalar=-float(CAP), in1=RANK, op0=ALU.mult, op1=ALU.add))
                for k, oh in enumerate((OH1, OH2)):
                    st.then(v.tensor_tensor(MSK, RANK, oh, ALU.mult))
                    st.then(v.tensor_reduce(small[:, 5, :], MSK, AX.X, ALU.add))
                    st.did(v.tensor_tensor(SLOT_R[:, k, 0:T, :], row(count, CAP), b3(small[:, 5, :], CAP), ALU.is_equal))
                    st.then(v.tensor_tensor(MSK, T1, oh, ALU.mult))
                    st.then(v.tensor_reduce(small[:, 6, :], MSK, AX.X, ALU.add))
                    blocks = SLOT_B[:, k, 0:T, :]
                    st.then(v.tensor_tensor(blocks, row(count[:, 0:NB], NB), b3(small[:, 6, :], NB), ALU.is_equal))
                    v.tensor_tensor(blocks, blocks, b3(entry[:, k, 0:T], NB), ALU.mult).then_inc(S("slot_rows"), 1)
                big = OF[:, 2048:2048 + 16 * NE].rearrange("p (b e) -> p b e", b=16)
                st.then(v.tensor_tensor(big, END.unsqueeze(1).to_broadcast([P, 16, NE]),
                                        iota[:, 0:16].unsqueeze(2).to_broadcast([P, 16, NE]), ALU.is_le))
                st.then(v.tensor_reduce(ov[:, 0, 0:16], big, AX.X, ALU.add))
                st.then(v.tensor_scalar(ov[:, 0, 0:16], ov[:, 0, 0:16], float(NE - 1), None, ALU.min))
                st.did(v.tensor_copy(OVI[0:1, l, 0:16], ov[0:1, 0, 0:16]))
                st.settle()
                v.tensor_copy(OVI[0:1, l, 16:17], END[0:1, NE - 1:NE]).then_inc(S("routed"), 1)
                wait(ve, "table", l, 1)
                st.then(v.tensor_scalar(OF[0:CAP, 5120:5120 + NB], PB[0:CAP, 7, 0:NB], float(EMPTY), None, ALU.add))
                st.then(v.tensor_copy(IDX[0:CAP, :], OF[0:CAP, 5120:5120 + NB]))
                v.tensor_scalar(IDT[0:CAP, :], IDX[0:CAP, :], 1, None, ALU.arith_shift_right).then_inc(S("tokens"), 1)

            def experts(l):
                def x_t(e, u, s_t, s_out, n):
                    wait(ve, s_t, l, n)
                    v.tensor_copy(XT[u][:, 4:8, 0:CAP], PB[:, 5, :].rearrange("p (k n) -> p k n", k=4)[:, :, 0:CAP]).then_inc(S(s_out), 1)

                def gate(u, n, s_sg, s_up, n_up, s_hx):
                    wait(ve, s_sg, l, n)
                    wait(ve, s_up, l, n_up)
                    v.tensor_tensor(HX[u], SG[u], PB[:, 2 * u + 1, 0:4 * CAP].rearrange("p (f n) -> p f n", f=4), ALU.mult).then_inc(S(s_hx), 1)

                def y_out(u, s_down, n, s_out):
                    wait(ve, s_down, l, n)
                    v.tensor_copy(YS[u][0:CAP, 512:1024], PB[0:CAP, 7, 0:512]).then_inc(S(s_out), 1)

                def main_x(e, u):
                    x_t(e, u, "xgT", "xTd", e + 1)

                def main_g(e, u):
                    gate(u, e + 1, "sg", "up_free", e + 3, "hx")

                def main_y(e, u, first=False):
                    if not first:
                        wait(ve, f"y_stored{u}", l, (e - u) * 8)
                    y_out(u, "down_free", e + 3, "y_d")
                main_x(0, 0)
                main_x(1, 1)
                main_g(0, 0)
                main_x(2, 0)
                main_g(1, 1)
                main_y(0, 0, True)
                main_x(3, 1)
                main_g(2, 0)
                main_y(1, 1, True)
                with ve.Fori(1, NE // 2 - 1) as i:
                    for u in (1, 0):
                        e = i * 2 + (1 if u else 2)
                        main_x(e + 1, 1 - u)
                        main_g(e, u)
                        main_y(e - 1, 1 - u)
                main_g(NE - 1, 1)
                main_y(NE - 2, 0)
                main_y(NE - 1, 1)
                def over_block(b, q):
                    x_t(q, 0, "over_xgT", "over_xTd", q + 1)
                    gate(0, q + 1, "over_sg", "over_up", q + 1, "over_hx")
                    y_out(0, "over_free", q + 2 + l, "over_yd")
                    lone_wait(ve, S("over_block"), q + 1)
                overflow(ve, l, over_block)

            def stage_f(l):
                wait(ve, "rowsf", l, 64)
                tl = tiles_of[l]

                def front(n, t):
                    m = m_of(t)
                    wait(ve, "y_scaled", l, n + 1)
                    y0, y1 = YG[n % 2][:, 0, :], YG[n % 2][:, 1, :]
                    st.then(v.scalar_tensor_tensor(out=y0, in0=y1, scalar=GATE[:, 1, n:n + 1], in1=y0, op0=ALU.mult, op1=ALU.add))
                    st.then(v.tensor_tensor(y0, y0, ROWS[:, ROW_G + m, :], ALU.mult))
                    v.scalar_tensor_tensor(out=X[:, t, :], in0=X[:, t, :], scalar=ALPHA, in1=y0, op0=ALU.mult, op1=ALU.add
                                           ).then_inc(S("yg_used"), 1)

                def stats(n, t):
                    wait(ve, "yg_used", l, n + 1)
                    if n:
                        wait(ve, "lnf_done", l, n)
                    for h in range(2):
                        st.did(v.bn_stats(BN[:, h, :], X[:, t, 512 * h:512 * (h + 1)]))
                    st.settle()
                    st.then(v.bn_aggr(MV[:, 2:4], BN[:, :, :].rearrange("p a b -> p (a b)")))
                    v.tensor_scalar(MV[:, 1:2], MV[:, 3:4], EPS, None, ALU.add).then_inc(S("lnf_ms"), 1)

                def move(n):
                    wait(ve, "lnf_root", l, n + 1)
                    v.tensor_scalar(MV[:, 0:1], MV[:, 2:3], MV[:, 1:2], -1.0, ALU.mult, ALU.mult).then_inc(S("lnf_moved"), 1)

                def back(n, t):
                    wait(ve, "lnf_done", l, n + 1)
                    if l == 0:
                        wait(ve, "xT", 1, n + 1)
                    st.then(v.tensor_tensor(X[:, t, :], X[:, t, :], ROWS[:, ROW_LG, :], ALU.mult))
                    v.tensor_tensor(X[:, t, :], X[:, t, :], ROWS[:, ROW_LB, :], ALU.add).then_inc(S("x_new"), 1)

                for n, t in enumerate(tl):
                    front(n, t)
                    stats(n, t)
                    if n and l:
                        back(n - 1, tl[n - 1])
                    move(n)
                for n in range(len(tl) - 1 if l else 0, len(tl)):
                    back(n, tl[n])

            def loop(ph, per, body):
                with ve.Fori(0, ph.iters) as i:
                    st.enter(i, per)
                    body(i)
                st.leave(ph.iters)

            def a_body(i):
                for t in range(NT):
                    rope(PA, i, t, 0, 4, False)
                attention(PA, i, lambda i, s: i * P)

            def b_body(i):
                attention(PBB, i, lambda i, s: i * HD + 512 + 256 * s)

            loop(PA, NT * 3 + NT * 2, a_body)
            st.did(v.memset(BK[HD:P, 0, :], 0.0))
            st.then(v.memset(BK[0:HD, 1, :], 0.0))
            for t in range(NT):
                rope(KV, 0, t, 2, 2, True)
            ve.wait_ge(S("kv_rope"), NT)
            for t in range(NT):
                rope(QP, 0, t, 1, 8, True)
            loop(PBB, 12, b_body)
            stage_c(0)
            routing(0)
            experts(0)
            clear_q()
            stage_f(0)

            def n_body(i):
                ve.wait_ge(S("bias"), (i + 1) * 6)
                attention(PN, i, lambda i, s: i * P + HD * s)
            loop(PN, PN.nu * 2, n_body)
            stage_c(1)
            routing(1)
            experts(1)
            stage_f(1)


_INS = ["x", "c", "ctx", "c_ctx", "w_mod", "b_mod", "ln_g", "ln_b", "w_in_even", "w_out_even", "diff_lam", "diff_subln_g",
        "gqa_qk_g", "w_in_odd", "w_out_odd", "na_rpb", "router_g", "router_e", "w1", "w3", "w2"]


def shape_constants():
    import numpy as np

    c = np.zeros((P, C_W), np.float32)
    c[:, C_ID:C_ID + P] = np.eye(P)
    c[:, C_TRI:C_TRI + P] = np.triu(np.ones((P, P)), 1)
    c[:, C_ONE:C_ONE + P] = 1.0
    c[:, C_COUNT:C_COUNT + CAP] = np.arange(CAP)
    for k in range(2):
        c[:, C_ENTRY + NT * k:C_ENTRY + NT * (k + 1)] = 2 * (np.arange(P)[:, None] + P * np.arange(NT)[None, :]) + k - EMPTY
    c[:, C_PRIO:C_PRIO + NE] = NE - np.arange(NE)
    c[:, C_PRIO4:C_PRIO4 + NG] = NG - np.arange(NG)
    col = np.arange(P)[:, None] // ROWS_N
    key = np.arange(32)[None, :]
    c[:, C_MASK:C_MASK + 32] = np.where((key >= col) & (key < col + WIN_W), 0.0, BIG_NEG)
    c[:, C_SEL:C_SEL + 4] = np.array([1.0, 0.0, 0.0, 1.0])
    c[:, C_MASK + 32:C_MASK + 34] = np.where(np.arange(2)[None, :] == np.arange(P)[:, None] // 64, 0.0, BIG_NEG)
    t = np.arange(SEQ)
    half = HD // 2
    inv = (np.float32(10000.0) ** (-np.arange(0, half, 2, dtype=np.float32) / np.float32(half))).astype(np.float32)
    ar = (t // GRID_W).astype(np.float32)[:, None] * inv
    ac = (t % GRID_W).astype(np.float32)[:, None] * inv
    ang = np.concatenate([ar, ar, ac, ac], -1)
    sign = np.repeat(np.array([-1, 1, -1, 1], np.float32), HD // 4)
    rope = np.zeros((P, NT, 2, HD), np.float32)
    rope[:, :NCT, 0, :] = 1.0
    order = np.concatenate([np.arange(8), np.arange(GRID_W - 8, GRID_W), np.arange(8, GRID_W - 8)])
    ang = ang[(np.arange(ROWS_N)[None, :] * GRID_W + order[:, None]).reshape(-1)]
    rope[:, NCT:, 0, :] = np.cos(ang).reshape(SEQ // P, P, HD).transpose(1, 0, 2)
    rope[:, NCT:, 1, :] = (np.sin(ang) * sign).reshape(SEQ // P, P, HD).transpose(1, 0, 2)
    return {"consts": c, "rope": rope}


def kernel(**inputs):
    import numpy as np
    import concourse.bacc as bacc
    from concourse.bass_utils import run_bass_kernel_spmd

    nc = bacc.Bacc("TRN2", target_bir_lowering=False, num_devices=1)
    arrays = {n: np.ascontiguousarray(inputs[n]) for n in _INS}
    arrays.update(shape_constants())
    aps = {n: nc.dram_tensor(f"in_{n}", list(a.shape), mybir.dt.from_np(a.dtype), kind="ExternalInput").ap() for n, a in arrays.items()}
    out = nc.dram_tensor("out", [1, SEQ, D], mybir.dt.float32, kind="ExternalOutput").ap()
    build(nc, aps, out)
    r = run_bass_kernel_spmd(nc, [{f"in_{n}": a for n, a in arrays.items()}], core_ids=[0])
    return r.results[0]["out"]
```
